# Optimizing a Trainium2 kernel written in Bass

```python
import math
import jax, jax.numpy as jnp
from jax import lax
import numpy as np

D_MODEL = 2048
BATCH = 1
SEQ = 256
DEPTH = 1

D_MIX = D_MODEL
D_CONV = D_MIX // 2
D_ATT = D_MIX - D_CONV
HEAD_DIM = 64
N_HEADS = D_ATT // HEAD_DIM
CONV_WIDTH = 31
IDX_HEADS = 16
IDX_DIM = 64
TOPK_MAX = 256
Q_BLOCK = 128
REL_BUCKETS = 32
REL_MAX_DIST = 128
PEER_HEADS = 8
PEER_KEYS = 128
PEER_N = PEER_KEYS * PEER_KEYS
PEER_DKEY = 256
PEER_TOPK = 16
PEER_BLOCK = 128
LN_EPS = 1e-5
ALPHA = (2.0 * DEPTH) ** 0.25
BETA = (8.0 * DEPTH) ** -0.25

COL_GLU = 2 * D_CONV
COL_Q = D_ATT
COL_K = D_ATT
COL_V = D_ATT
COL_QIDX = IDX_HEADS * IDX_DIM
COL_KIDX = IDX_DIM
COL_WIDX = IDX_HEADS
D_IN = COL_GLU + COL_Q + COL_K + COL_V + COL_QIDX + COL_KIDX + COL_WIDX
SPLITS = (COL_GLU,
          COL_GLU + COL_Q,
          COL_GLU + COL_Q + COL_K,
          COL_GLU + COL_Q + COL_K + COL_V,
          COL_GLU + COL_Q + COL_K + COL_V + COL_QIDX,
          COL_GLU + COL_Q + COL_K + COL_V + COL_QIDX + COL_KIDX)

kernel_name = "hymba_conformer_dsa_peer_deepnorm"

def layer_norm(x, g, b):
    xf = x.astype(jnp.float32)
    mu = jnp.mean(xf, axis=-1, keepdims=True)
    var = jnp.mean(jnp.square(xf - mu), axis=-1, keepdims=True)
    return ((xf - mu) * lax.rsqrt(var + LN_EPS) * g.astype(jnp.float32)
            + b.astype(jnp.float32)).astype(x.dtype)

def rel_bucket(dist):
    max_exact = REL_BUCKETS // 2
    d = jnp.maximum(dist, 0)
    large = max_exact + (jnp.log(jnp.maximum(d, 1).astype(jnp.float32) / max_exact)
                         / math.log(REL_MAX_DIST / max_exact)
                         * (REL_BUCKETS - max_exact)).astype(jnp.int32)
    large = jnp.minimum(large, REL_BUCKETS - 1)
    return jnp.where(d < max_exact, d, large)

def conv_group(a, dw_w, dw_b, cn_g, cn_b):
    h = a[..., :D_CONV] * jax.nn.sigmoid(a[..., D_CONV:])
    h = lax.conv_general_dilated(
        h, dw_w[:, None, :].astype(h.dtype), window_strides=(1,),
        padding=[(CONV_WIDTH - 1, 0)],
        dimension_numbers=('NWC', 'WIO', 'NWC'),
        feature_group_count=D_CONV) + dw_b
    h = layer_norm(h, cn_g, cn_b)
    return jax.nn.silu(h)

def dsa_attention(q, k, v, q_idx, k_idx, w_idx, rel_bias):
    B, S = q.shape[0], q.shape[1]
    n_sel = min(TOPK_MAX, S // 4)
    n_blocks = S // Q_BLOCK
    key_pos = jnp.arange(S, dtype=jnp.int32)
    scale = HEAD_DIM ** -0.5

    def block(i):
        t0 = i * Q_BLOCK
        qb = lax.dynamic_slice_in_dim(q, t0, Q_BLOCK, axis=1)
        qib = lax.dynamic_slice_in_dim(q_idx, t0, Q_BLOCK, axis=1)
        wb = lax.dynamic_slice_in_dim(w_idx, t0, Q_BLOCK, axis=1)
        q_pos = t0 + jnp.arange(Q_BLOCK, dtype=jnp.int32)
        causal = key_pos[None, :] <= q_pos[:, None]
        rel = jax.nn.relu(jnp.einsum('bthd,bsd->bths', qib, k_idx))
        score = jnp.einsum('bths,bth->bts', rel, wb).astype(jnp.float32)
        score = jnp.where(causal[None], score, -jnp.inf)
        _, sel = lax.top_k(score, n_sel)
        kg = jax.vmap(lambda kk, ii: kk[ii])(k, sel)
        vg = jax.vmap(lambda vv, ii: vv[ii])(v, sel)
        logits = jnp.einsum('bthd,btkhd->bhtk', qb, kg).astype(jnp.float32) * scale
        dist = q_pos[None, :, None] - sel
        bias = rel_bias.astype(jnp.float32)[rel_bucket(dist)]
        logits = logits + jnp.transpose(bias, (0, 3, 1, 2))
        logits = jnp.where((dist >= 0)[:, None], logits, -jnp.inf)
        p = jax.nn.softmax(logits, axis=-1).astype(v.dtype)
        return jnp.einsum('bhtk,btkhd->bthd', p, vg)

    out = lax.map(block, jnp.arange(n_blocks, dtype=jnp.int32))
    return jnp.transpose(out, (1, 0, 2, 3, 4)).reshape(B, S, N_HEADS * HEAD_DIM)

def peer(x, w_q, sub_keys, u_tab, v_tab):
    B, S, D = x.shape
    n_tok = B * S
    xt = x.reshape(n_tok, D)
    q = (xt @ w_q).reshape(n_tok, PEER_HEADS, 2, PEER_DKEY // 2)
    s = jnp.einsum('nhcd,hckd->nhck', q, sub_keys).astype(jnp.float32)
    s1, i1 = lax.top_k(s[:, :, 0], PEER_TOPK)
    s2, i2 = lax.top_k(s[:, :, 1], PEER_TOPK)
    cand_s = (s1[..., :, None] + s2[..., None, :]).reshape(n_tok, PEER_HEADS, PEER_TOPK * PEER_TOPK)
    cand_i = (i1[..., :, None] * PEER_KEYS + i2[..., None, :]).reshape(n_tok, PEER_HEADS, PEER_TOPK * PEER_TOPK)
    top_s, pos = lax.top_k(cand_s, PEER_TOPK)
    experts = jnp.take_along_axis(cand_i, pos, axis=-1)
    gates = jax.nn.softmax(top_s, axis=-1).astype(x.dtype)
    n_blocks = n_tok // PEER_BLOCK

    def block(i):
        t0 = i * PEER_BLOCK
        xb = lax.dynamic_slice_in_dim(xt, t0, PEER_BLOCK, axis=0)
        eb = lax.dynamic_slice_in_dim(experts, t0, PEER_BLOCK, axis=0)
        gb = lax.dynamic_slice_in_dim(gates, t0, PEER_BLOCK, axis=0)
        ub = u_tab[eb]
        h = jax.nn.gelu(jnp.einsum('td,thed->the', xb, ub), approximate=False)
        vb = v_tab[eb]
        return jnp.einsum('the,thed->td', gb * h, vb)

    out = lax.map(block, jnp.arange(n_blocks, dtype=jnp.int32))
    return out.reshape(B, S, D)

def setup_inputs(seed: int = 0) -> dict:
    key = jax.random.key(seed)
    ks = jax.random.split(key, 24)
    f32 = jnp.float32
    sd = D_MODEL ** -0.5

    def nrm(k, shape, s):
        return jax.random.normal(k, shape, f32) * s

    x = jax.random.normal(ks[0], (BATCH, SEQ, D_MODEL), f32)
    w_in = jnp.concatenate([
        nrm(ks[1], (DEPTH, D_MODEL, COL_GLU), sd),
        nrm(ks[2], (DEPTH, D_MODEL, COL_Q), sd),
        nrm(ks[3], (DEPTH, D_MODEL, COL_K), sd),
        nrm(ks[4], (DEPTH, D_MODEL, COL_V), sd * BETA),
        nrm(ks[5], (DEPTH, D_MODEL, COL_QIDX), sd),
        nrm(ks[6], (DEPTH, D_MODEL, COL_KIDX), sd),
        nrm(ks[7], (DEPTH, D_MODEL, COL_WIDX), sd),
    ], axis=-1)
    w_out = nrm(ks[8], (DEPTH, D_MIX, D_MODEL), BETA * D_MIX ** -0.5)
    b_out = nrm(ks[9], (DEPTH, D_MODEL), 0.01)
    dw_w = nrm(ks[10], (DEPTH, CONV_WIDTH, D_CONV), CONV_WIDTH ** -0.5)
    dw_b = nrm(ks[11], (DEPTH, D_CONV), 0.01)
    conv_ln_g = 1.0 + nrm(ks[12], (DEPTH, D_CONV), 0.01)
    conv_ln_b = nrm(ks[13], (DEPTH, D_CONV), 0.01)
    rel_bias = nrm(ks[14], (REL_BUCKETS, N_HEADS), 0.5)
    ln1_g = 1.0 + nrm(ks[15], (DEPTH, D_MODEL), 0.01)
    ln1_b = nrm(ks[16], (DEPTH, D_MODEL), 0.01)
    peer_wq = nrm(ks[17], (DEPTH, D_MODEL, PEER_HEADS * PEER_DKEY), sd)
    peer_sub_keys = nrm(ks[18], (DEPTH, PEER_HEADS, 2, PEER_KEYS, PEER_DKEY // 2), (PEER_DKEY // 2) ** -0.5)
    peer_u = nrm(ks[19], (DEPTH, PEER_N, D_MODEL), sd)
    peer_v = nrm(ks[20], (DEPTH, PEER_N, D_MODEL), BETA)
    ln2_g = 1.0 + nrm(ks[21], (DEPTH, D_MODEL), 0.01)
    ln2_b = nrm(ks[22], (DEPTH, D_MODEL), 0.01)
    return {"x": x, "w_in": w_in, "w_out": w_out, "b_out": b_out,
            "dw_w": dw_w, "dw_b": dw_b, "conv_ln_g": conv_ln_g, "conv_ln_b": conv_ln_b,
            "rel_bias": rel_bias, "ln1_g": ln1_g, "ln1_b": ln1_b,
            "peer_wq": peer_wq, "peer_sub_keys": peer_sub_keys,
            "peer_u": peer_u, "peer_v": peer_v, "ln2_g": ln2_g, "ln2_b": ln2_b}

def reference(x, w_in, w_out, b_out, dw_w, dw_b, conv_ln_g, conv_ln_b, rel_bias,
              ln1_g, ln1_b, peer_wq, peer_sub_keys, peer_u, peer_v, ln2_g, ln2_b):
    B, S, _ = x.shape
    for l in range(DEPTH):
        proj = x @ w_in[l]
        a_glu, q, k, v, q_idx, k_idx, w_idx = jnp.split(proj, SPLITS, axis=-1)
        conv_out = conv_group(a_glu, dw_w[l], dw_b[l], conv_ln_g[l], conv_ln_b[l])
        att_out = dsa_attention(
            q.reshape(B, S, N_HEADS, HEAD_DIM),
            k.reshape(B, S, N_HEADS, HEAD_DIM),
            v.reshape(B, S, N_HEADS, HEAD_DIM),
            q_idx.reshape(B, S, IDX_HEADS, IDX_DIM), k_idx, w_idx, rel_bias)
        mix = jnp.concatenate([conv_out, att_out], axis=-1) @ w_out[l] + b_out[l]
        x = layer_norm(ALPHA * x + mix, ln1_g[l], ln1_b[l])
        y = peer(x, peer_wq[l], peer_sub_keys[l], peer_u[l], peer_v[l])
        x = layer_norm(ALPHA * x + y, ln2_g[l], ln2_b[l])
    return x


_drawn_inputs = setup_inputs


def setup_inputs(seed=0):
    import zlib

    import numpy as np

    out = dict(_drawn_inputs(seed))
    spreads = {}
    factors = {'dw_b': 3.054, 'conv_ln_g': 4.06, 'conv_ln_b': 4.456, 'ln2_g': 5.523, 'ln2_b': 5.651}
    for name, (base, spread) in spreads.items():
        noise = np.random.default_rng([zlib.crc32(name.encode()), seed]).standard_normal(out[name].shape)
        drawn = base * np.exp(spread * noise) if base else spread * noise
        out[name] = __import__('jax').numpy.asarray(drawn.astype(out[name].dtype))
    for name, factor in factors.items():
        out[name] = (out[name] * factor).astype(out[name].dtype)
    return out
```

```python
from contextlib import ExitStack

import concourse.bass as bass
import numpy as np
from concourse import mybir

F32 = mybir.dt.float32
I32 = mybir.dt.int32
U32 = mybir.dt.uint32
ALU = mybir.AluOpType
ACT = mybir.ActivationFunctionType
AX = mybir.AxisListType

P = 128
D = 2048
S = 256
TI = S // P
KC = D // P
DC = D // 2
CC = DC // P
TAPS = 31
HD = 64
NH = 16
NSEL = 64
BUCKETS = 32
MAX_DIST = 128
PH = 8
PK = 128
TOP = 16
SLOTS = PH * TOP
EPS = 1e-5
ALPHA = 2.0 ** 0.25
NEG = -1.0e30
FILL = -1.0e37
TAKEN = -3.0e38

UNIT = 2048
RING = 4
U_IDX, U_GLU, U_V, U_QK, U_OUT, U_WQ, U_END = 0, 8, 24, 32, 48, 64, 80
KWCOL = P + NH
SKEW = S + P - 1

G = 4
RG = 2
GROUPS = SLOTS // G


def layer(nc, xT, x_tok, w_stream, w_kw, w_sub, conv_p, cln, bucket1h, rel_bias,
          b_out, ln1_col, ln_rows, u_tab, v_tab, out):
    with ExitStack() as ctx:
        def sb(name, shape, dt=F32):
            return ctx.enter_context(nc.sbuf_tensor(name, shape, dt))

        def sem(name):
            return ctx.enter_context(nc.semaphore(name))

        psum = ctx.enter_context(nc.psum_tensor("psum", [P, 8, 512], F32))
        ps = [psum[:, i, :] for i in range(8)]

        def span(i):
            return slice(0, S) if i else slice(S, S + P)

        region = sb("region", [P, 2 * RG * G * D])
        place = [0]

        def part(cols):
            place[0] += cols
            assert place[0] <= 2 * RG * G * D
            return region[:, place[0] - cols:place[0]]

        scratch = sb("scratch", [P, 6560])
        at = {"attention": 0, "peer": 0}

        def tmp(half, cols):
            at[half] += cols
            assert at[half] <= 6560
            return scratch[:, at[half] - cols:at[half]]

        x_cols = part(KC * S)
        xT_sb = x_cols.rearrange("p (c t) -> p c t", c=KC)
        ring = [part(UNIT) for _ in range(RING)]
        bias = part(NH * S).rearrange("p (h s) -> p h s", h=NH)
        v_sb = part(TI * DC).rearrange("p (b c) -> p b c", b=TI)
        att = part(TI * DC).rearrange("p (i c) -> p i c", i=TI)
        cat_cols = part(2 * CC * S)
        catT = cat_cols.rearrange("p (c t) -> p c t", c=2 * CC)
        skew = cat_cols.rearrange("p (h s) -> p h s", h=NH)
        conv_cols = part(CC * S)
        convT = conv_cols.rearrange("p (c t) -> p c t", c=CC)
        sq_cols = part(CC * S)
        kw_cols = part(KC * KWCOL)
        kw = kw_cols.rearrange("p (c n) -> p c n", c=KC)
        sub = kw_cols[:, 0:2 * PH * PK]
        b_row = sq_cols[0:1, :]
        u_ring = [region[:, k * D:(k + 1) * D] for k in range(RG * G)]
        v_ring = [region[:, (RG * G + k) * D:(RG * G + k + 1) * D] for k in range(RG * G)]

        x1 = sb("x1", [P, TI, D])
        rows = sb("ln_rows_sb", [P, 2, D])

        ident = sb("ident", [P, P])
        ident_a = sb("ident_alpha", [P, P])
        flip = sb("flip", [P, P])
        mean_w = sb("mean_w", [P, P])
        ones_row = sb("ones_row", [1, P])
        iota_i = sb("iota_i", [P, TI * TOP * TOP], I32)
        iota_f = sb("iota_f", [P, TI * TOP * TOP])
        onehot = sb("onehot", [BUCKETS, SKEW])
        relb = sb("relb", [BUCKETS, NH])
        dist_row = sb("dist_row", [NH, SKEW])
        conv_sb = sb("conv_sb", [P, CC * (TAPS + 1)])
        conv_c = sb("conv_c", [P, TAPS + 1])
        cln_sb = sb("cln_sb", [P, 2 * CC])
        ln1c = sb("ln1c", [P, 2 * KC])
        eps = sb("eps", [P, 1])

        kidxT = sb("kidxT", [P, S])
        widx = sb("widx", [P, TI * NH])
        qidx = [tmp("attention", S) for k in range(2)]
        rel = [tmp("attention", 2 * (S + P)).rearrange("p (j s) -> p j s", j=2) for k in range(2)]
        acc = [tmp("attention", P), tmp("attention", S)]
        acc_b = [tmp("attention", P), tmp("attention", S)]
        best8 = [sb("best8_0", [P, 8]), sb("best8_1", [P, 8])]
        mask = [tmp("attention", P), tmp("attention", S)]
        sig = [tmp("attention", S) for k in range(2)]
        cbuf = tmp("attention", TAPS - 1 + S)
        cacc = tmp("attention", S)
        rstd_c = tmp("attention", S)
        qT = tmp("attention", S)
        kT = tmp("attention", S)
        lg = [tmp("attention", 2 * P).rearrange("p (j s) -> p j s", j=2), tmp("attention", 2 * S).rearrange("p (j s) -> p j s", j=2)]
        mx = sb("mx", [P, 4])
        nm = sb("nm", [P, 4])
        rsum = [sb(f"rsum{k}", [P, 4]) for k in range(2)]
        rinv = sb("rinv", [P, 4])
        pT = [tmp("attention", 2 * P), tmp("attention", 4 * P)]
        stats = sb("stats", [P, TI * 4, 6])
        mv = sb("mv", [P, TI, 2])
        sd = sb("sd", [P, TI])
        rstd = sb("rstd", [P, TI])

        qc = [tmp("peer", S) for k in range(2)]
        sw = [tmp("peer", TI * PK).rearrange("p (i k) -> p i k", i=TI) for k in range(2)]
        sw2 = tmp("peer", TI * PK).rearrange("p (i k) -> p i k", i=TI)
        val = [sb(f"val{c}", [P, TI, TOP]) for c in range(2)]
        idx = [sb(f"idx{c}", [P, TI, TOP], U32) for c in range(2)]
        idxf = [sb(f"idxf{c}", [P, TI, TOP]) for c in range(2)]
        cand = tmp("peer", TI * TOP * TOP).rearrange("p (i k) -> p i k", i=TI)
        cand2 = tmp("peer", TI * TOP * TOP).rearrange("p (i k) -> p i k", i=TI)
        pos = sb("pos", [P, TI, TOP], U32)
        posp = [sb(f"posp{c}", [P, TI * TOP], U32) for c in range(2)]
        posf = [sb(f"posf{c}", [P, TI * TOP]) for c in range(2)]
        pick = [sb(f"pick{c}", [P, TI * TOP]) for c in range(2)]
        hit = [tmp("peer", TI * TOP * TOP).rearrange("p (r j) -> p r j", j=TOP) for c in range(2)]
        gate = sb("gate", [P, TI, SLOTS])
        gsum = sb("gsum", [P, TI * PH])
        ginv = sb("ginv", [P, TI * PH])
        eid = sb("eid", [P, TI, SLOTS], I32)
        eslot = [sb(f"eslot{k}", [P, G], I32) for k in range(RG)]
        dots = [sb(f"dots{k}", [P, G]) for k in range(RG)]
        gel = [sb(f"gel{k}", [P, G]) for k in range(RG)]
        diag = [tmp("peer", G * P).rearrange("p (j t) -> p j t", j=G) for k in range(RG)]

        row_scratch = nc.dram_tensor("dist_rows", (NH, SKEW), F32, kind="Internal").ap()

        x_in, kw_in, small_in, row_in, sub_in, b_in, row2_in = (
            sem(n) for n in ("x_in", "kw_in", "small_in", "row_in", "sub_in", "b_in", "row2_in"))
        w_in = [sem(f"w_in{k}") for k in range(RING)]
        row_out, skew_in = sem("row_out"), sem("skew_in")
        out_done = sem("out_done")
        pool_const = sem("pool_const")
        causal = sem("causal")
        dve_step = sem("dve_step")
        w_used = sem("w_used")
        kw_done, kw_copied = sem("kw_done"), sem("kw_copied")
        qidx_copied, score_done, relu_done, idx_added = (sem(n) for n in ("qidx_copied", "score_done", "relu_done", "idx_added"))
        row_done, row_copied, flip_done, bias_copied = (sem(n) for n in ("row_done", "row_copied", "flip_done", "bias_copied"))
        iota_done = sem("iota_done")
        scored, masked = sem("scored"), sem("masked")
        sig_done, glu_done, conv_done = sem("sig_done"), sem("glu_done"), sem("conv_done")
        v_copied = sem("v_copied")
        mean_done, centred, squared, var_done, sd_done, normed, conv_out = (
            sem(n) for n in ("mean_done", "centred", "squared", "var_done", "sd_done", "normed", "conv_out"))
        qk_copied, logit_done, logit_read, max_done, exp_done = (
            sem(n) for n in ("qk_copied", "logit_done", "logit_read", "max_done", "exp_done"))
        turned, pt_copied, pv_done, att_done = sem("turned"), sem("pt_copied"), sem("pv_done"), sem("att_done")
        att_turned, att_copied, mix_read = sem("att_turned"), sem("att_copied"), sem("mix_read")
        var1, sd1, xn_done, xn_turned, x1T_done, x1_done = (
            sem(n) for n in ("var1", "sd1", "xn_done", "xn_turned", "x1T_done", "x1_done"))
        qc_copied, key_done, key_copied, key_used = (sem(n) for n in ("qc_copied", "key_done", "key_copied", "key_used"))
        gate_sub, gate_exp, picked = sem("gate_sub"), sem("gate_exp"), sem("picked")
        eslot_done = sem("eslot_done")
        u_in = [sem(f"u_in{k}") for k in range(RG * G)]
        v_in = [sem(f"v_in{k}") for k in range(RG * G)]
        dots_done, gelu_done, diag_done, y_done = (sem(n) for n in ("dots_done", "gelu_done", "diag_done", "y_done"))
        var2, sd2, res_done = sem("var2"), sem("sd2"), sem("res_done")
        passed = {e: sem(f"passed_{e}") for e in ("pe", "act", "dve", "pool")}

        block = ctx.enter_context(nc.Block())

        @block.sync
        def _(sp):
            for q in range(4):
                sp.dma_start(xT_sb[:, 4 * q:4 * q + 4, :], xT[:, 4 * q:4 * q + 4, :]).then_inc(x_in, 16)
            sp.dma_start(kw, w_kw).then_inc(kw_in, 16)
            for k in range(RING):
                sp.dma_start(ring[k], w_stream[k]).then_inc(w_in[k], 16)
            with sp.Fori(1, U_END // RING) as r:
                for k in range(RING):
                    sp.wait_ge(w_used, r * RING + (k - RING + 1))
                    sp.dma_start(ring[k], w_stream[bass.ds(r * RING + k, 1)].rearrange("a p n -> (a p) n")).then_inc(w_in[k], 16)
            for i in range(TI):
                sp.wait_ge(res_done, i + 1)
                sp.dma_start(out[i * P:(i + 1) * P, :], x1[:, i, :]).then_inc(out_done, 16)
            sp.wait_ge(out_done, 16 * TI)

        @block.gpsimd
        def _(pool):
            pool.memset(ident[:, :], 0.0)
            pool.memset(ident_a[:, :], 0.0)
            pool.memset(flip[:, :], 0.0)
            pool.memset(mean_w[:, :], 1.0 / DC)
            pool.memset(ones_row[:, :], 1.0)
            pool.memset(eps[:, :], EPS)
            pool.iota(iota_i[:, :].rearrange("p (r j) -> p r j", j=TOP), [[0, TI * TOP], [1, TOP]], channel_multiplier=0).then_inc(pool_const, 1)
            pool.wait_ge(pool_const, 1)
            pool.affine_select(out=ident[:, :], in_=ident[:, :], compare_op=ALU.not_equal, fill=1.0,
                               base=0, pattern=[[-1, P]], channel_multiplier=1)
            pool.affine_select(out=ident_a[:, :], in_=ident_a[:, :], compare_op=ALU.not_equal, fill=ALPHA,
                               base=0, pattern=[[-1, P]], channel_multiplier=1)
            pool.affine_select(out=flip[:, :], in_=flip[:, :], compare_op=ALU.not_equal, fill=1.0,
                               base=-(P - 1), pattern=[[1, P]], channel_multiplier=1).then_inc(pool_const, 1)
            pool.wait_ge(w_used, 2)
            pool.dma_start(x1[:, :, :], x_tok.rearrange("(i p) d -> p i d", p=P)).then_inc(row_in, 16)
            for k in range(2):
                pool.dma_start(rows[:, k, :], ln_rows[k:k + 1, :].to_broadcast([P, D])).then_inc(row_in, 16)
            pool.dma_start(sub[:, :], w_sub).then_inc(sub_in, 16)
            for i in range(TI):
                pool.wait_ge(scored, i + 1)
                pool.affine_select(out=acc[i][:, :], in_=acc[i][:, :], compare_op=ALU.is_ge, fill=FILL,
                                   base=i * P, pattern=[[-1, (i + 1) * P]], channel_multiplier=1).then_inc(causal, 1)
            for i in range(TI):
                pool.wait_ge(masked, i + 1)
                pool.affine_select(out=mask[i][:, :], in_=mask[i][:, :], compare_op=ALU.is_ge, fill=NEG,
                                   base=i * P, pattern=[[-1, (i + 1) * P]], channel_multiplier=1).then_inc(causal, 1)

            pool.wait_ge(var_done, 1)
            pool.dma_start(b_row, b_out).then_inc(b_in, 16)
            pool.wait_ge(x1_done, TI)
            for k in range(2):
                pool.dma_start(rows[:, k, :], ln_rows[k + 2:k + 3, :].to_broadcast([P, D])).then_inc(row2_in, 16)

            pool.wait_ge(picked, 1)
            for i in range(TI):
                with pool.Fori(0, GROUPS // RG) as r:
                    for k in range(RG):
                        g = r * RG + (k + i * GROUPS)
                        pool.wait_ge(dots_done, g + 1)
                        pool.wait_ge(y_done, g + 1)
                        pool.sem_inc(passed["pool"], 1)
                        pool.tensor_copy(eslot[k][:, :], eid[:, i, bass.ds((r * RG + k) * G, G)]).then_inc(eslot_done, 1)
                        pool.wait_ge(eslot_done, g + 1)
                        pool.sem_inc(passed["pool"], 1)
                        for tab, dst, land in ((u_tab, u_ring, u_in), (v_tab, v_ring, v_in)):
                            for j in range(G):
                                pool.indirect_dma_start(
                                    dst[k * G + j], None, tab,
                                    bass.IndirectOffsetOnAxis(ap=eslot[k][:, j:j + 1], axis=0),
                                ).then_inc(land[k * G + j], 16)

        @block.tensor
        def _(pe):
            def unit_in(u, k):
                pe.wait_ge(w_in[k], (u - k) * (16 // RING) + 16)

            def project(u, k, dst, cols):
                unit_in(u, k)
                w = ring[k].rearrange("p (c n) -> p c n", c=KC)
                for c in range(KC):
                    last = pe.matmul(dst, w[:, c, :], cols[:, c, :], start=c == 0, stop=c == KC - 1)
                last.then_inc(w_used, 1)

            pe.wait_ge(small_in, 16 * 6)
            pe.matmul(ps[7][0:NH, 0:SKEW], relb[:, :], onehot[:, :], start=True, stop=True).then_inc(row_done, 1)
            pe.wait_ge(x_in, 64)
            pe.wait_ge(kw_in, 16)
            for c in range(KC):
                pe.matmul(ps[0][:, 0:S], kw[:, c, 0:P], xT_sb[:, c, :], start=c == 0, stop=c == KC - 1)
            for i in range(TI):
                for c in range(KC):
                    last = pe.matmul(ps[1][:, i * NH:(i + 1) * NH], xT_sb[:, c, i * P:(i + 1) * P], kw[:, c, P:KWCOL],
                                     start=c == 0, stop=c == KC - 1)
            last.then_inc(kw_done, 1)
            pe.wait_ge(kw_copied, 2)

            def index_scores(u, k):
                pe.wait_ge(qidx_copied, u + 3)
                pe.wait_ge(relu_done, u + 1)
                for i in range(TI):
                    for j in range(2):
                        n = (i + 1) * P
                        last = pe.matmul(ps[2 + 2 * j + k % 2][:, span(i)],
                                         qidx[k % 2][j * HD:(j + 1) * HD, i * P:(i + 1) * P],
                                         kidxT[j * HD:(j + 1) * HD, 0:n], start=True, stop=True)
                last.then_inc(score_done, 1)

            with pe.Fori(0, CC // RING) as r:
                for k in range(RING):
                    u = r * RING + k
                    pe.wait_ge(qidx_copied, u + 1)
                    project(u, k, ps[k % 2][:, 0:S], xT_sb)
                    if k:
                        index_scores(u - 1, k - 1)
                index_scores(r * RING + (RING - 1), RING - 1)

            pe.wait_ge(skew_in, 16)
            pe.wait_ge(pool_const, 2)
            for n in range(8):
                pe.wait_ge(bias_copied, max(n - 1, 0))
                pe.matmul(ps[6 + n % 2][:, :], flip[:, :], cat_cols[:, n * 512:(n + 1) * 512],
                          start=True, stop=True).then_inc(flip_done, 1)

            pe.wait_ge(relu_done, CC + 2)
            with pe.Fori(0, CC // 2) as r:
                for k in range(2):
                    pe.wait_ge(glu_done, r * 2 + (k + 1))
                    for part_ in range(2):
                        s = 2 * k + part_
                        project(r * RING + (U_GLU + s), s, ps[s][:, 0:S], xT_sb)

            pe.wait_ge(bias_copied, 8)
            for n in range(2):
                for q in range(RING):
                    unit_in(U_V + n * RING + q, q)
                    w = ring[q].rearrange("p (c n) -> p c n", c=4)
                    for c in range(4):
                        for i in range(TI):
                            last = pe.matmul(ps[4 + 2 * n + i][:, :], xT_sb[:, 4 * q + c, i * P:(i + 1) * P], w[:, c, :],
                                             start=q + c == 0, stop=q + c == 6)
                    last.then_inc(w_used, 1)

            pe.wait_ge(conv_done, CC)
            pe.wait_ge(v_copied, 4)
            for c in range(CC):
                last = pe.matmul(ps[7][:, 0:S], mean_w[:, :], convT[:, c, :], start=c == 0, stop=c == CC - 1)
            last.then_inc(mean_done, 1)

            def qk(hp, k):
                pe.wait_ge(qk_copied, hp * 2)
                project(hp * 2 + U_QK, 2 * k, ps[0][:, 0:S], xT_sb)
                project(hp * 2 + (U_QK + 1), 2 * k + 1, ps[1][:, 0:S], xT_sb)

            def logits(hp):
                pe.wait_ge(qk_copied, hp * 2 + 2)
                pe.wait_ge(logit_read, hp)
                for i in range(TI):
                    n = (i + 1) * P
                    for j in range(2):
                        last = pe.matmul(ps[2 + j][:, span(i)], qT[j * HD:(j + 1) * HD, i * P:(i + 1) * P],
                                         kT[j * HD:(j + 1) * HD, 0:n], start=True, stop=True)
                last.then_inc(logit_done, 1)

            def turn(hp):
                pe.wait_ge(exp_done, hp * 4 + 4)
                for i in range(TI):
                    for j in range(2):
                        for b in range(i + 1):
                            last = pe.transpose(ps[4 + i][:, (j * (i + 1) + b) * P:(j * (i + 1) + b + 1) * P],
                                                lg[i][:, j, b * P:(b + 1) * P], ident[:, :])
                last.then_inc(turned, 1)

            def values(hp):
                pe.wait_ge(pt_copied, hp * 2 + 2)
                pe.wait_ge(att_done, hp + 1)
                for i in range(TI):
                    for j in range(2):
                        for b in range(i + 1):
                            last = pe.matmul(ps[6][:, (2 * i + j) * HD:(2 * i + j + 1) * HD],
                                             pT[i][:, (j * (i + 1) + b) * P:(j * (i + 1) + b + 1) * P],
                                             v_sb[:, b, bass.ds(hp * P + j * HD, HD)], start=b == 0, stop=b == i)
                last.then_inc(pv_done, 1)

            pe.wait_ge(glu_done, CC + 2)
            qk(0, 0)
            logits(0)
            pe.wait_ge(squared, 1)
            for c in range(CC):
                last = pe.matmul(ps[7][:, 0:S], mean_w[:, :], sq_cols[:, c * S:(c + 1) * S], start=c == 0, stop=c == CC - 1)
            last.then_inc(var_done, 1)
            with pe.Fori(0, 3) as r:
                for k in range(2):
                    hp = r * 2 + (k + 1)
                    qk(hp, 1 - k)
                    turn(hp - 1)
                    logits(hp)
                    values(hp - 1)
            qk(7, 1)
            turn(6)
            logits(7)
            values(6)
            turn(7)
            values(7)

            pe.wait_ge(att_done, CC + 1)
            for m in range(4):
                for c in range(2):
                    for i in range(TI):
                        last = pe.transpose(ps[2 + m][:, (2 * c + i) * P:(2 * c + i + 1) * P],
                                            att[:, i, (2 * m + c) * P:(2 * m + c + 1) * P], ident[:, :])
                last.then_inc(att_turned, 1)

            pe.wait_ge(b_in, 16)
            for n in range(4):
                bank = 6 if n % 2 else 0
                pe.wait_ge(mix_read, max(n - 1, 0) * TI)
                for i in range(TI):
                    pe.matmul(ps[bank + i][:, :], ones_row[:, :], b_row[:, n * 512:(n + 1) * 512], start=True, stop=False)
                for q in range(RING):
                    unit_in(U_OUT + n * RING + q, q)
                    if n == 0 and q == 0:
                        pe.wait_ge(conv_out, CC)
                    if n == 0 and q == 2:
                        pe.wait_ge(att_copied, 4)
                    w = ring[q].rearrange("p (c n) -> p c n", c=4)
                    for c in range(4):
                        for i in range(TI):
                            last = pe.matmul(ps[bank + i][:, :], catT[:, 4 * q + c, i * P:(i + 1) * P], w[:, c, :],
                                             start=False, stop=q + c == 6)
                    last.then_inc(w_used, 1)

            pe.wait_ge(xn_done, 2)
            for m in range(KC // 2):
                pe.wait_ge(x1T_done, max(2 * (m - 3), 0))
                for c in range(2):
                    for i in range(TI):
                        last = pe.transpose(ps[2 + m % 4][:, (2 * c + i) * P:(2 * c + i + 1) * P],
                                            x1[:, i, (2 * m + c) * P:(2 * m + c + 1) * P], ident[:, :])
                last.then_inc(xn_turned, 1)

            def key_scores(u, k):
                pe.wait_ge(qc_copied, u + 3)
                pe.wait_ge(key_copied, u + 1)
                for i in range(TI):
                    last = pe.matmul(ps[2 + k % 2][:, i * PK:(i + 1) * PK], qc[k % 2][:, i * P:(i + 1) * P],
                                     sub[:, bass.ds(u * PK, PK)], start=True, stop=True)
                last.then_inc(key_done, 1)

            pe.wait_ge(x1T_done, KC)
            pe.wait_ge(mix_read, 8)
            pe.wait_ge(sub_in, 16)
            with pe.Fori(0, 2 * PH // RING) as r:
                for k in range(RING):
                    u = r * RING + k
                    pe.wait_ge(qc_copied, u + 1)
                    project(u + U_WQ, k, ps[k % 2][:, 0:S], xT_sb)
                    if k:
                        key_scores(u - 1, k - 1)
                key_scores(r * RING + (RING - 1), RING - 1)

            for i in range(TI):
                pe.wait_ge(x1_done, i + 1)
                if i == 0:
                    pe.wait_ge(key_copied, 2 * PH + 2)
                for n in range(4):
                    pe.matmul(ps[4 * i + n][:, :], ident_a[:, :], x1[:, i, n * 512:(n + 1) * 512], start=True, stop=False,
                              skip_group_check=True)
                with pe.Fori(0, GROUPS // RG) as r:
                    for k in range(RG):
                        g = r * RG + (k + i * GROUPS)
                        pe.wait_ge(diag_done, g + 1)
                        for j in range(G):
                            pe.wait_ge(v_in[k * G + j], r * 16 + (16 + 16 * i * GROUPS // RG))
                            for n in range(4):
                                last = pe.matmul(ps[4 * i + n][:, :], diag[k][:, j, :], v_ring[k * G + j][:, n * 512:(n + 1) * 512],
                                                 start=False, stop=True, skip_group_check=True)
                        last.then_inc(y_done, 1)

        @block.scalar
        def _(act):
            act.dma_start(relb[:, :], rel_bias).then_inc(small_in, 16)
            act.dma_start(onehot[:, :], bucket1h).then_inc(small_in, 16)
            act.dma_start(conv_sb[:, :], conv_p).then_inc(small_in, 16)
            act.dma_start(cln_sb[:, :], cln).then_inc(small_in, 16)
            act.dma_start(ln1c[:, 0:KC], ln1_col[0]).then_inc(small_in, 16)
            act.dma_start(ln1c[:, KC:2 * KC], ln1_col[1]).then_inc(small_in, 16)
            act.sem_inc(qidx_copied, 2)
            act.sem_inc(relu_done, 2)
            act.sem_inc(qc_copied, 2)
            act.sem_inc(key_copied, 2)
            act.wait_ge(row_done, 1)
            act.activation(dist_row[:, :], ps[7][0:NH, 0:SKEW], ACT.Copy).then_inc(row_copied, 1)
            act.wait_ge(row_copied, 1)
            act.dma_start(row_scratch, dist_row[:, :]).then_inc(row_out, 16)
            act.wait_ge(row_out, 16)
            act.dma_start(skew, bass.AP(tensor=row_scratch.tensor, offset=0, ap=[[1, P], [SKEW, NH], [1, S]])).then_inc(skew_in, 16)

            act.wait_ge(kw_done, 1)
            act.activation(kidxT[:, :], ps[0][:, 0:S], ACT.Copy).then_inc(kw_copied, 1)
            act.activation(widx[:, :], ps[1][:, 0:TI * NH], ACT.Copy).then_inc(kw_copied, 1)

            def relu(u):
                b = u % 2
                act.wait_ge(score_done, u + 1)
                if u >= 2:
                    act.wait_ge(idx_added, u - 1)
                for j in range(2):
                    last = act.activation(rel[b][:, j, :], ps[2 + 2 * j + b][:, 0:S + P], ACT.Relu)
                last.then_inc(relu_done, 1)

            for u in range(CC):
                act.wait_ge(w_used, U_IDX + u + 1)
                if u >= 2:
                    act.wait_ge(score_done, u - 1)
                act.activation(qidx[u % 2][:, :], ps[u % 2][:, 0:S], ACT.Copy).then_inc(qidx_copied, 1)
                if u % RING:
                    relu(u - 1)
                if u % RING == RING - 1:
                    relu(u)

            for n in range(8):
                act.wait_ge(flip_done, n + 1)
                act.activation(bias[:, 2 * n:2 * n + 2, :].rearrange("p h s -> p (h s)"), ps[6 + n % 2][:, :], ACT.Copy).then_inc(bias_copied, 1)

            for c in range(CC):
                act.wait_ge(w_used, U_GLU + 2 * c + 2)
                if c >= 2:
                    act.wait_ge(glu_done, c - 1 + 2)
                act.activation(sig[c % 2][:, :], ps[2 * (c % 2) + 1][:, 0:S], ACT.Sigmoid).then_inc(sig_done, 1)

            for n in range(2):
                act.wait_ge(w_used, U_V + RING * (n + 1))
                for i in range(TI):
                    act.activation(v_sb[:, i, n * 512:(n + 1) * 512], ps[4 + 2 * n + i][:, :], ACT.Copy).then_inc(v_copied, 1)

            act.wait_ge(centred, 1)
            act.activation(sq_cols, conv_cols, ACT.Square).then_inc(squared, 1)

            def qk_copy(hp):
                act.wait_ge(w_used, hp * 2 + (U_QK + 1))
                act.wait_ge(logit_done, hp)
                act.activation(qT[:, :], ps[0][:, 0:S], ACT.Copy, scale=HD ** -0.5).then_inc(qk_copied, 1)
                act.wait_ge(w_used, hp * 2 + (U_QK + 2))
                act.activation(kT[:, :], ps[1][:, 0:S], ACT.Copy).then_inc(qk_copied, 1)

            def exps(hp, b):
                act.wait_ge(max_done, hp + 1)
                for i in range(TI):
                    for j in range(2):
                        a = 2 * i + j
                        act.activation(lg[i][:, j, :], lg[i][:, j, :], ACT.Exp, bias=nm[:, a:a + 1],
                                       accum_out=rsum[b][:, a:a + 1]).then_inc(exp_done, 1)

            def pt_copy(hp):
                act.wait_ge(turned, hp + 1)
                act.wait_ge(pv_done, hp + 1)
                act.activation(pT[0][:, :], ps[4][:, 0:2 * P], ACT.Copy).then_inc(pt_copied, 1)
                act.activation(pT[1][:, :], ps[5][:, :], ACT.Copy).then_inc(pt_copied, 1)

            qk_copy(0)
            exps(0, 0)
            act.wait_ge(var_done, 1)
            act.activation(rstd_c[:, :], ps[7][:, 0:S], ACT.Sqrt, bias=eps[:, :]).then_inc(sd_done, 1)
            act.wait_ge(normed, 1)
            for c in range(CC):
                act.activation(catT[:, c, :], convT[:, c, :], ACT.Silu, scale=cln_sb[:, c:c + 1],
                               bias=cln_sb[:, CC + c:CC + c + 1]).then_inc(conv_out, 1)
            with act.Fori(0, 3) as r:
                for k in range(2):
                    hp = r * 2 + (k + 1)
                    qk_copy(hp)
                    pt_copy(hp - 1)
                    exps(hp, 1 - k)
            qk_copy(7)
            pt_copy(6)
            exps(7, 1)
            pt_copy(7)

            for m in range(4):
                act.wait_ge(att_turned, m + 1)
                act.activation(catT[:, CC + 2 * m:CC + 2 * m + 2, :].rearrange("p c t -> p (c t)"), ps[2 + m][:, :], ACT.Copy).then_inc(att_copied, 1)

            act.wait_ge(var1, 1)
            act.activation(sd[:, :], mv[:, :, 1], ACT.Sqrt, bias=eps[:, :]).then_inc(sd1, 1)
            for m in range(KC // 2):
                act.wait_ge(xn_turned, m + 1)
                for c in range(2):
                    kc = 2 * m + c
                    act.activation(xT_sb[:, kc, :], ps[2 + m % 4][:, c * S:(c + 1) * S], ACT.Identity,
                                   scale=ln1c[:, kc:kc + 1], bias=ln1c[:, KC + kc:KC + kc + 1]).then_inc(x1T_done, 1)

            def key_copy(u):
                act.wait_ge(key_done, u + 1)
                if u >= 2:
                    act.wait_ge(key_used, u - 1)
                act.activation(sw[u % 2][:, :, :].rearrange("p i k -> p (i k)"), ps[2 + u % 2][:, 0:TI * PK], ACT.Copy).then_inc(key_copied, 1)

            for u in range(2 * PH):
                act.wait_ge(w_used, U_WQ + u + 1)
                if u >= 2:
                    act.wait_ge(key_done, u - 1)
                act.activation(qc[u % 2][:, :], ps[u % 2][:, 0:S], ACT.Copy).then_inc(qc_copied, 1)
                if u % RING:
                    key_copy(u - 1)
                if u % RING == RING - 1:
                    key_copy(u)

            act.wait_ge(gate_sub, 1)
            act.activation(gate[:, :, :], gate[:, :, :], ACT.Exp).then_inc(gate_exp, 1)

            def gelus(first, last, i):
                with act.Fori(first, last) as r:
                    for k in range(RG):
                        act.wait_ge(dots_done, r * RG + (k + i * GROUPS + 1 + RG))
                        act.activation(gel[k][:, :], dots[k][:, :], ACT.Gelu).then_inc(gelu_done, 1)

            def sd_rows(i):
                act.wait_ge(var2, i + 1)
                act.activation(sd[:, i:i + 1], mv[:, i, 1:2], ACT.Sqrt, bias=eps[:, :]).then_inc(sd2, 1)

            gelus(0, GROUPS // RG, 0)
            gelus(0, 2, 1)
            sd_rows(0)
            gelus(2, GROUPS // RG, 1)
            sd_rows(1)

        @block.vector
        def _(dve):
            steps = [0]

            def link(ins):
                steps[0] += 1
                ins.then_inc(dve_step, 1)
                dve.wait_ge(dve_step, steps[0])

            dve.sem_inc(glu_done, 2)
            dve.sem_inc(dots_done, RG)
            dve.sem_inc(y_done, RG)
            dve.sem_inc(att_done, 1)
            dve.sem_inc(pv_done, 1)
            dve.memset(cbuf[:, :], 0.0)
            for i in range(TI):
                dve.memset(acc[i][:, :], 0.0)
            dve.wait_ge(pool_const, 1)
            link(dve.tensor_copy(iota_f[:, :], iota_i[:, :]))

            dve.wait_ge(kw_copied, 2)
            for u in range(CC):
                dve.wait_ge(relu_done, 2 + u + 1)
                for j in range(2):
                    for i in range(TI):
                        h = i * NH + 2 * u + j
                        last = dve.scalar_tensor_tensor(out=acc[i][:, :], in0=rel[u % 2][:, j, span(i)], scalar=widx[:, h:h + 1],
                                                        in1=acc[i][:, :], op0=ALU.mult, op1=ALU.add)
                    if j == 0:
                        link(last)
                last.then_inc(idx_added, 1)
                dve.wait_ge(idx_added, u + 1)
            for i in range(TI):
                dve.sem_inc(scored, 1)
            dve.wait_ge(causal, TI)
            a, b = acc, acc_b
            for n in range(NSEL // 8):
                for i in range(TI):
                    last = dve.max(best8[i][:, :], a[i][:, :])
                link(last)
                for i in range(TI):
                    last = dve.match_replace(b[i][:, :], best8[i][:, :], a[i][:, :], TAKEN)
                link(last)
                a, b = b, a
            for i in range(TI):
                dve.tensor_scalar(mask[i][:, :], a[i][:, :], TAKEN / 2, NEG, ALU.is_gt, ALU.mult).then_inc(masked, 1)

            dve.wait_ge(small_in, 16 * 6)
            for c in range(CC):
                dve.wait_ge(sig_done, c + 1)
                dve.tensor_copy(conv_c[:, :], conv_sb[:, c * (TAPS + 1):(c + 1) * (TAPS + 1)])
                dve.tensor_tensor(cbuf[:, TAPS - 1:], ps[2 * (c % 2)][:, 0:S], sig[c % 2][:, :], ALU.mult).then_inc(glu_done, 1)
                dve.wait_ge(glu_done, c + 3)
                link(dve.tensor_scalar(cacc[:, :], cbuf[:, 0:S], conv_c[:, 0:1], conv_c[:, TAPS:TAPS + 1], ALU.mult, ALU.add))
                for t in range(1, TAPS - 1):
                    link(dve.scalar_tensor_tensor(out=cacc[:, :], in0=cbuf[:, t:t + S], scalar=conv_c[:, t:t + 1],
                                                  in1=cacc[:, :], op0=ALU.mult, op1=ALU.add))
                dve.scalar_tensor_tensor(out=convT[:, c, :], in0=cbuf[:, TAPS - 1:], scalar=conv_c[:, TAPS - 1:TAPS],
                                         in1=cacc[:, :], op0=ALU.mult, op1=ALU.add).then_inc(conv_done, 1)
                dve.wait_ge(conv_done, c + 1)

            dve.wait_ge(mean_done, 1)
            for c in range(CC):
                last = dve.tensor_tensor(convT[:, c, :], convT[:, c, :], ps[7][:, 0:S], ALU.subtract)
            last.then_inc(centred, 1)

            def softmax_in(hp):
                dve.wait_ge(logit_done, hp + 1)
                for i in range(TI):
                    last = dve.tensor_tensor(lg[i][:, :, :], psum[:, 2:4, span(i)],
                                             bias[:, 2 * hp:2 * hp + 2, P - i * P:S], ALU.add)
                last.then_inc(logit_read, 1)
                dve.wait_ge(logit_read, hp + 1)
                for i in range(TI):
                    for j in range(2):
                        last = dve.tensor_tensor_reduce(lg[i][:, j, :], lg[i][:, j, :], mask[i][:, :], 1.0, -3.4e38,
                                                        ALU.add, ALU.max, mx[:, 2 * i + j:2 * i + j + 1])
                link(last)
                dve.tensor_scalar(nm[:, :], mx[:, :], -1.0, None, ALU.mult).then_inc(max_done, 1)

            def heads_out(hp):
                dve.wait_ge(pv_done, hp + 2)
                link(dve.reciprocal(rinv[:, :], rsum[hp % 2][:, :]))
                dve.tensor_tensor(att[:, :, hp * P:(hp + 1) * P].rearrange("p i (j d) -> p i j d", j=2),
                                  ps[6][:, 0:4 * HD].rearrange("p (i j d) -> p i j d", i=2, j=2),
                                  rinv[:, :].rearrange("p (i j o) -> p i j o", i=2, o=1).to_broadcast([P, 2, 2, HD]),
                                  ALU.mult).then_inc(att_done, 1)

            dve.wait_ge(bias_copied, 8)
            dve.wait_ge(causal, 2 * TI)
            softmax_in(0)
            dve.wait_ge(sd_done, 1)
            link(dve.reciprocal(cacc[:, :], rstd_c[:, :]))
            dve.wait_ge(squared, 1)
            for c in range(CC):
                last = dve.tensor_tensor(convT[:, c, :], convT[:, c, :], cacc[:, :], ALU.mult)
            last.then_inc(normed, 1)
            for hp in range(1, CC):
                softmax_in(hp)
                heads_out(hp - 1)
            heads_out(CC - 1)

            dve.wait_ge(row_in, 16 * 3)
            for n in range(4):
                dve.wait_ge(w_used, U_OUT + RING * (n + 1))
                for i in range(TI):
                    x_n = x1[:, i, n * 512:(n + 1) * 512]
                    dve.scalar_tensor_tensor(out=x_n, in0=x_n, scalar=ALPHA, in1=ps[(6 if n % 2 else 0) + i][:, :],
                                             op0=ALU.mult, op1=ALU.add).then_inc(mix_read, 1)
                dve.wait_ge(mix_read, TI * (n + 1))
                for i in range(TI):
                    last = dve.bn_stats(stats[:, 4 * i + n, :], x1[:, i, n * 512:(n + 1) * 512])
            link(last)
            for i in range(TI):
                last = dve.bn_aggr(mv[:, i, :], stats[:, 4 * i:4 * i + 4, :])
            last.then_inc(var1, 1)
            dve.wait_ge(sd1, 1)
            link(dve.reciprocal(rstd[:, :], sd[:, :]))
            for i in range(TI):
                dve.tensor_scalar(x1[:, i, :], x1[:, i, :], mv[:, i, 0:1], rstd[:, i:i + 1], ALU.subtract, ALU.mult).then_inc(xn_done, 1)
            dve.wait_ge(xn_turned, KC // 2)
            for i in range(TI):
                last = dve.tensor_tensor(x1[:, i, :], x1[:, i, :], rows[:, 0, :], ALU.mult)
            link(last)
            for i in range(TI):
                dve.tensor_tensor(x1[:, i, :], x1[:, i, :], rows[:, 1, :], ALU.add).then_inc(x1_done, 1)

            def top16(vals, ids, src, tmp):
                for i in range(TI):
                    last = dve.max(vals(i)[:, 0:8], src[:, i, :])
                link(last)
                for i in range(TI):
                    dve.max_index(ids[:, i, 0:8], vals(i)[:, 0:8], src[:, i, :])
                    last = dve.match_replace(tmp[:, i, :], vals(i)[:, 0:8], src[:, i, :], TAKEN)
                link(last)
                for i in range(TI):
                    last = dve.max(vals(i)[:, 8:16], tmp[:, i, :])
                link(last)
                for i in range(TI):
                    last = dve.max_index(ids[:, i, 8:16], vals(i)[:, 8:16], tmp[:, i, :])
                return last

            iota_v = iota_f[:, :].rearrange("p (r j) -> p r j", j=TOP)
            for u in range(2 * PH):
                h, c = u // 2, u % 2
                dve.wait_ge(key_copied, 2 + u + 1)
                top16(lambda i: val[c][:, i, :], idx[c], sw[u % 2], sw2).then_inc(key_used, 1)
                dve.wait_ge(key_used, u + 1)
                if c == 0:
                    continue
                link(dve.tensor_tensor(cand[:, :, :].rearrange("p i (a b) -> p i a b", a=TOP),
                                       val[0][:, :, :].rearrange("p i (a o) -> p i a o", o=1).to_broadcast([P, TI, TOP, TOP]),
                                       val[1][:, :, :].rearrange("p i (o b) -> p i o b", o=1).to_broadcast([P, TI, TOP, TOP]), ALU.add))
                link(top16(lambda i: gate[:, i, h * TOP:(h + 1) * TOP], pos, cand, cand2))
                pos_v = pos[:, :, :].rearrange("p i r -> p (i r)")
                dve.tensor_scalar(posp[0][:, :], pos_v, 4, None, ALU.logical_shift_right)
                dve.tensor_scalar(posp[1][:, :], pos_v, TOP - 1, None, ALU.bitwise_and)
                for q in range(2):
                    last = dve.tensor_copy(idxf[q][:, :, :], idx[q][:, :, :])
                link(last)
                for q in range(2):
                    last = dve.tensor_copy(posf[q][:, :], posp[q][:, :])
                link(last)
                for q in range(2):
                    last = dve.tensor_tensor(hit[q][:, :, :], posf[q][:, :].rearrange("p (r o) -> p r o", o=1).to_broadcast([P, TI * TOP, TOP]),
                                             iota_v, ALU.is_equal)
                link(last)
                for q in range(2):
                    hit_v = hit[q][:, :, :].rearrange("p (i r) j -> p i r j", i=TI)
                    last = dve.tensor_tensor(hit_v, hit_v, idxf[q][:, :, :].rearrange("p i (o j) -> p i o j", o=1).to_broadcast([P, TI, TOP, TOP]), ALU.mult)
                link(last)
                for q in range(2):
                    last = dve.tensor_reduce(pick[q][:, :], hit[q][:, :, :], AX.X, ALU.add)
                link(last)
                link(dve.scalar_tensor_tensor(out=eid[:, :, h * TOP:(h + 1) * TOP], in0=pick[0][:, :].rearrange("p (i r) -> p i r", i=TI),
                                              scalar=float(PK), in1=pick[1][:, :].rearrange("p (i r) -> p i r", i=TI),
                                              op0=ALU.mult, op1=ALU.add))
            dve.sem_inc(picked, 1)
            gate_v = gate[:, :, :].rearrange("p i (h r) -> p (i h) r", h=PH)
            link(dve.tensor_copy(gsum[:, :], gate_v[:, :, 0]))
            dve.tensor_tensor(gate_v, gate_v, gsum[:, :].rearrange("p (a o) -> p a o", o=1).to_broadcast([P, TI * PH, TOP]),
                              ALU.subtract).then_inc(gate_sub, 1)
            dve.wait_ge(gate_exp, 1)
            link(dve.tensor_reduce(gsum[:, :], gate_v, AX.X, ALU.add))
            link(dve.reciprocal(ginv[:, :], gsum[:, :]))
            link(dve.tensor_tensor(gate_v, gate_v, ginv[:, :].rearrange("p (a o) -> p a o", o=1).to_broadcast([P, TI * PH, TOP]), ALU.mult))

            def experts(first, last, i):
                with dve.Fori(first, last) as r:
                    for k in range(RG):
                        g = r * RG + (k + i * GROUPS)
                        for j in range(G):
                            s = k * G + j
                            dve.wait_ge(u_in[s], r * 16 + (16 + 16 * i * GROUPS // RG))
                            ins = dve.tensor_tensor_reduce(u_ring[s], u_ring[s], x1[:, i, :], 1.0, 0.0,
                                                           ALU.mult, ALU.add, dots[k][:, j:j + 1])
                        ins.then_inc(dots_done, 1)
                        dve.wait_ge(gelu_done, g + 1)
                        dve.wait_ge(y_done, g + 1)
                        for j in range(G):
                            ins = dve.tensor_scalar(diag[k][:, j, :], ident[:, :], gel[k][:, j:j + 1],
                                                    gate[:, i, bass.ds((r * RG + k) * G + j, 1)], ALU.mult, ALU.mult)
                        ins.then_inc(diag_done, 1)

            def norm_out(i):
                dve.wait_ge(y_done, RG + GROUPS * (i + 1))
                for n in range(4):
                    last = dve.bn_stats(stats[:, n, :], ps[4 * i + n][:, :])
                link(last)
                dve.bn_aggr(mv[:, i, :], stats[:, 0:4, :]).then_inc(var2, 1)
                dve.wait_ge(sd2, i + 1)
                link(dve.reciprocal(rstd[:, i:i + 1], sd[:, i:i + 1]))
                res = x1[:, i, :]
                dve.wait_ge(row2_in, 32)
                for n in range(4):
                    last = dve.tensor_scalar(res[:, n * 512:(n + 1) * 512], ps[4 * i + n][:, :], mv[:, i, 0:1], rstd[:, i:i + 1],
                                             ALU.subtract, ALU.mult)
                link(last)
                link(dve.tensor_tensor(res, res, rows[:, 0, :], ALU.mult))
                dve.tensor_tensor(res, res, rows[:, 1, :], ALU.add).then_inc(res_done, 1)

            experts(0, GROUPS // RG, 0)
            experts(0, 2, 1)
            norm_out(0)
            experts(2, GROUPS // RG, 1)
            norm_out(1)


def _bucket_onehot():
    half = BUCKETS // 2
    d = np.maximum(S - 1 - np.arange(SKEW), 0)
    large = half + (np.log(np.maximum(d, 1).astype(np.float32) / np.float32(half))
                    / np.float32(np.log(MAX_DIST / half)) * np.float32(BUCKETS - half)).astype(np.int32)
    b = np.where(d < half, d, np.minimum(large, BUCKETS - 1))
    return (np.arange(BUCKETS)[:, None] == b[None, :]).astype(np.float32)


def kernel(x, w_in, w_out, b_out, dw_w, dw_b, conv_ln_g, conv_ln_b, rel_bias,
           ln1_g, ln1_b, peer_wq, peer_sub_keys, peer_u, peer_v, ln2_g, ln2_b):
    import concourse.bacc as _bacc
    from concourse.bass_utils import run_bass_kernel_spmd as _run

    def tiles(w):
        return np.asarray(w).reshape(KC, P, -1, P).transpose(2, 1, 0, 3).reshape(-1, P, UNIT)

    def strips(w):
        return np.asarray(w).reshape(4, 4, P, -1, 512).transpose(3, 0, 2, 1, 4).reshape(-1, P, UNIT)

    def pair(a, b):
        return np.stack([tiles(a), tiles(b)], 1).reshape(-1, P, UNIT)

    def cols(v, n):
        return np.asarray(v).reshape(n, P).T

    w = np.asarray(w_in)[0]
    c_q, c_k, c_v, c_qi, c_ki, c_wi = 2 * DC, 3 * DC, 4 * DC, 5 * DC, 6 * DC, 6 * DC + HD
    stream = np.concatenate([tiles(w[:, c_qi:c_ki]), pair(w[:, 0:DC], w[:, DC:2 * DC]), strips(w[:, c_v:c_qi]),
                             pair(w[:, c_q:c_k], w[:, c_k:c_v]), strips(np.asarray(w_out)[0]), tiles(np.asarray(peer_wq)[0])])
    k_i, w_i = w[:, c_ki:c_wi], w[:, c_wi:]
    kw = np.concatenate([k_i, k_i, w_i], 1).reshape(KC, P, KWCOL).transpose(1, 0, 2)
    x2 = np.asarray(x)[0]
    conv = np.concatenate([np.asarray(dw_w)[0], np.asarray(dw_b)], 0)
    ins = {
        "xT": x2.T.reshape(KC, P, S).transpose(1, 0, 2),
        "x_tok": x2,
        "w_stream": stream,
        "w_kw": kw,
        "w_sub": np.asarray(peer_sub_keys)[0].transpose(3, 0, 1, 2).reshape(P, 2 * PH * PK),
        "conv_p": conv.reshape(TAPS + 1, CC, P).transpose(2, 1, 0).reshape(P, -1),
        "cln": np.concatenate([cols(conv_ln_g, CC), cols(conv_ln_b, CC)], 1),
        "bucket1h": _bucket_onehot(),
        "rel_bias": np.asarray(rel_bias),
        "b_out": np.asarray(b_out),
        "ln1_col": np.stack([cols(ln1_g, KC), cols(ln1_b, KC)]),
        "ln_rows": np.concatenate([np.asarray(a) for a in (ln1_g, ln1_b, ln2_g, ln2_b)], 0),
        "u_tab": np.asarray(peer_u)[0],
        "v_tab": np.asarray(peer_v)[0],
    }
    nc = _bacc.Bacc("TRN2", target_bir_lowering=False, num_devices=1)
    arrays, args = {}, {}
    for name, a in ins.items():
        a = np.ascontiguousarray(a)
        arrays[f"in_{name}"] = a
        args[name] = nc.dram_tensor(f"in_{name}", a.shape, mybir.dt.from_np(a.dtype), kind="ExternalInput").ap()
    args["out"] = nc.dram_tensor("out_dram", (S, D), F32, kind="ExternalOutput").ap()
    layer(nc, **args)
    r = _run(nc, [arrays], core_ids=[0])
    return r.results[0]["out_dram"].reshape(1, S, D)
```

```python
from contextlib import ExitStack

import concourse.bass as bass
import numpy as np
from concourse import mybir

F32 = mybir.dt.float32
I32 = mybir.dt.int32
U32 = mybir.dt.uint32
F32R = mybir.dt.float32r
ALU = mybir.AluOpType
ACT = mybir.ActivationFunctionType
AX = mybir.AxisListType

P = 128
D = 2048
S = 256
TI = S // P
KC = D // P
DC = D // 2
CC = DC // P
TAPS = 31
HD = 64
NH = 16
NSEL = 64
BUCKETS = 32
MAX_DIST = 128
PH = 8
PK = 128
TOP = 16
SLOTS = PH * TOP
EPS = 1e-5
ALPHA = 2.0 ** 0.25
NEG = -1.0e30
FILL = -1.0e37
TAKEN = -3.0e38

UNIT = 2048
RING = 4
U_IDX, U_GLU, U_V, U_QK, U_OUT, U_WQ, U_END = 0, 8, 24, 32, 48, 64, 80
KWCOL = P + NH
SKEW = S + P - 1

G = 4
RG = 2
GROUPS = SLOTS // G


def layer(nc, xT, x_tok, w_stream, w_kw, w_sub, conv_p, cln, bucket1h, rel_bias,
          b_out, ln1_col, ln_rows, u_tab, v_tab, out):
    with ExitStack() as ctx:
        def sb(name, shape, dt=F32):
            return ctx.enter_context(nc.sbuf_tensor(name, shape, dt))

        def sem(name):
            return ctx.enter_context(nc.semaphore(name))

        psum = ctx.enter_context(nc.psum_tensor("psum", [P, 8, 512], F32))
        ps = [psum[:, i, :] for i in range(8)]

        def span(i):
            return slice(0, S) if i else slice(S, S + P)

        KB = 1024
        arena0 = (nc.sbuf_base + 63) // 64 * 64
        arena = sb("arena", [P, (160 * KB + 64) // 4])
        spot = {"x_hi": 0, "x_lo": 16, "w_lo": 32, "w_hi": 64, "bias": 96, "cat_hi": 112, "rows": 128, "x1": 144}

        def put(name, where, shape, dt=F32, plus=0):
            return nc.alloc_sbuf_tensor_at(name, shape, dt, offset=arena0 + (spot[where] + plus) * KB)[:]

        xh = put("xT_hi", "x_hi", [P, KC, S], F32R)
        xl = put("xT_lo", "x_lo", [P, KC, S], F32R)
        b_row = put("b_row", "x_hi", [1, D])
        w_raw = [put(f"w_raw{k}", "w_lo", [P, UNIT], plus=8 * k) for k in range(RING)]
        w_lo = [put(f"w_lo{k}", "w_lo", [P, UNIT], F32R, plus=8 * k) for k in range(RING)]
        w_hi = [put(f"w_hi{k}", "w_hi", [P, UNIT], F32R, plus=8 * k) for k in range(RING)]
        x_raw = put("xT_raw", "bias", [P, KC, S])
        bias = put("bias", "bias", [P, NH, S])
        sub = put("sub", "bias", [P, 2 * PH * PK])
        x1c = [put(f"x1T_chunks{k}", "bias", [P, 2 * S], plus=8 + 2 * k) for k in range(4)]
        skew = put("skew", "cat_hi", [P, NH, S])
        sq = put("conv_sq", "cat_hi", [P, CC, S], plus=8)
        cat_h = put("catT_hi", "cat_hi", [P, 2 * CC, S], F32R)
        kw = put("kw", "rows", [P, KC, KWCOL])
        convT = put("convT", "rows", [P, CC, S], plus=8)
        cat_l = put("catT_lo", "rows", [P, 2 * CC, S], F32R)
        rows = put("ln_rows_sb", "rows", [P, 2, D])
        v_sb = put("v_sb", "x1", [P, TI, DC])
        att = put("att", "x1", [P, TI, DC], plus=8)
        x1 = put("x1", "x1", [P, TI, D])
        places = [("cat_hi", 0), ("cat_hi", 8)] + [("x_hi", 8 * k) for k in range(2 * RG * G - 2)]
        u_ring, v_ring = ([put(f"{n}_row{k}", w, [P, D], plus=o) for k, (w, o) in enumerate(part)]
                          for n, part in (("u", places[:RG * G]), ("v", places[RG * G:])))

        scratch = sb("scratch", [P, 4768])
        at = {"attention": 0, "peer": 0}

        def tmp(half, cols):
            at[half] += cols
            assert at[half] <= 4768
            return scratch[:, at[half] - cols:at[half]]

        ident = sb("ident", [P, P])
        ident_a = sb("ident_alpha", [P, P])
        flip = sb("flip", [P, P])
        mean_w = sb("mean_w", [P, P])
        ones_row = sb("ones_row", [1, P])
        iota_i = sb("iota_i", [P, TOP * TOP], I32)
        iota_f = sb("iota_f", [P, TOP * TOP])
        onehot = sb("onehot", [BUCKETS, SKEW])
        relb = sb("relb", [BUCKETS, NH])
        dist_row = sb("dist_row", [NH, SKEW])
        conv_sb = sb("conv_sb", [P, CC * (TAPS + 1)])
        conv_c = sb("conv_c", [P, TAPS + 1])
        cln_sb = sb("cln_sb", [P, 2 * CC])
        ln1c = sb("ln1c", [P, 2 * KC])
        eps = sb("eps", [P, 1])

        kidxT = sb("kidxT", [P, S])
        widx = sb("widx", [P, TI * NH])
        qidx = [tmp("attention", S) for k in range(2)]
        rel = [tmp("attention", 2 * (S + P)).rearrange("p (j s) -> p j s", j=2) for k in range(2)]
        acc = [tmp("attention", P), tmp("attention", S)]
        acc_b = [tmp("attention", P), tmp("attention", S)]
        best8 = [sb("best8_0", [P, 8]), sb("best8_1", [P, 8])]
        mask = [tmp("attention", P), tmp("attention", S)]
        sig = [tmp("attention", S) for k in range(2)] + qidx
        cbuf = tmp("attention", TAPS - 1 + S)
        cacc = [tmp("attention", S) for k in range(2)]
        rstd_c = tmp("attention", S)
        at["attention"] = 0
        qT = tmp("attention", S)
        kT = tmp("attention", S)
        lg = [tmp("attention", 2 * P).rearrange("p (j s) -> p j s", j=2), tmp("attention", 2 * S).rearrange("p (j s) -> p j s", j=2)]
        mx = sb("mx", [P, 4])
        nm = sb("nm", [P, 4])
        rsum = [sb(f"rsum{k}", [P, 4]) for k in range(2)]
        rinv = sb("rinv", [P, 4])
        pT = [tmp("attention", 2 * P), tmp("attention", 4 * P)]
        assert at["attention"] <= 2 * S + 4 * (S + P)
        stats = sb("stats", [P, TI * 4, 6])
        mv = sb("mv", [P, TI, 2])
        sd = sb("sd", [P, TI])
        rstd = sb("rstd", [P, TI])
        nmr = sb("minus_mean_rstd", [P, TI])

        qc = [tmp("peer", S) for k in range(2)]
        sw = [tmp("peer", PK) for k in range(4)]
        later = sb("later", [P, 2 * PH * PK])
        sw2 = [tmp("peer", PK) for c in range(2)]
        val = [sb(f"val{c}", [P, TOP]) for c in range(2)]
        idx = [sb(f"idx{c}", [P, TOP], U32) for c in range(2)]
        idxf = [sb(f"idxf{c}", [P, TOP]) for c in range(2)]
        cand = tmp("peer", TOP * TOP)
        cand2 = tmp("peer", TOP * TOP)
        pos = sb("pos", [P, TOP], U32)
        posp = [sb(f"posp{c}", [P, TOP], U32) for c in range(2)]
        posf = [sb(f"posf{c}", [P, TOP]) for c in range(2)]
        pick = [sb(f"pick{c}", [P, TOP]) for c in range(2)]
        hit = [tmp("peer", TOP * TOP).rearrange("p (r j) -> p r j", j=TOP) for c in range(2)]
        gate = sb("gate", [P, TI, SLOTS])
        gsum = sb("gsum", [P, PH])
        ginv = sb("ginv", [P, PH])
        eid = sb("eid", [P, TI, SLOTS], I32)
        eslot = [sb(f"eslot{k}", [P, G], I32) for k in range(RG)]
        dots = [sb(f"dots{k}", [P, G]) for k in range(RG)]
        gel = [sb(f"gel{k}", [P, G]) for k in range(RG)]
        diag = [tmp("peer", G * P).rearrange("p (j t) -> p j t", j=G) for k in range(RG)]

        row_scratch = nc.dram_tensor("dist_rows", (NH, SKEW), F32, kind="Internal").ap()

        x_split = sem("x_split")
        hi_done = sem("hi_done")
        lo_pool, lo_dve = sem("lo_pool"), sem("lo_dve")
        x_hi_done = sem("x_hi_done")
        att_lo, cat_lo, x1c_done, x1h_done = sem("att_lo"), sem("cat_lo"), sem("x1c_done"), sem("x1h_done")
        x_in = [sem(f"x_in{q}") for q in range(4)]
        kw_in = [sem(f"kw_in{q}") for q in range(4)]
        small_in, row_in, sub_in, b_in, row2_in = (
            sem(n) for n in ("small_in", "row_in", "sub_in", "b_in", "row2_in"))
        row1_in = sem("row1_in")
        w_in = [sem(f"w_in{k}") for k in range(RING)]
        row_out, skew_in = sem("row_out"), sem("skew_in")
        out_done = sem("out_done")
        pool_const = sem("pool_const")
        causal = sem("causal")
        dve_step = sem("dve_step")
        w_used = sem("w_used")
        kw_done, kw_copied = sem("kw_done"), sem("kw_copied")
        qidx_copied, score_done, relu_done, idx_added = (sem(n) for n in ("qidx_copied", "score_done", "relu_done", "idx_added"))
        row_done, row_copied, flip_done, bias_copied = (sem(n) for n in ("row_done", "row_copied", "flip_done", "bias_copied"))
        iota_done = sem("iota_done")
        scored, masked = sem("scored"), sem("masked")
        sig_done, glu_done, conv_done = sem("sig_done"), sem("glu_done"), sem("conv_done")
        v_copied = sem("v_copied")
        mean_done, centred, squared, var_done, sd_done, normed, conv_out = (
            sem(n) for n in ("mean_done", "centred", "squared", "var_done", "sd_done", "normed", "conv_out"))
        qk_copied, logit_done, logit_read, max_done, exp_done = (
            sem(n) for n in ("qk_copied", "logit_done", "logit_read", "max_done", "exp_done"))
        turned, pt_copied, pv_done, att_done = sem("turned"), sem("pt_copied"), sem("pv_done"), sem("att_done")
        att_turned, att_copied, mix_read = sem("att_turned"), sem("att_copied"), sem("mix_read")
        mix_done = sem("mix_done")
        var1, sd1, shift1, xn0_done, xn1_done, xn_turned, x1T_even, x1T_odd, x1_done = (
            sem(n) for n in ("var1", "sd1", "shift1", "xn0_done", "xn1_done", "xn_turned", "x1T_even", "x1T_odd", "x1_done"))
        qc_copied, key_done, key_copied, key_used = (sem(n) for n in ("qc_copied", "key_done", "key_copied", "key_used"))
        gate_sub, gate_exp, picked = sem("gate_sub"), sem("gate_exp"), sem("picked")
        eslot_done = sem("eslot_done")
        u_in = [sem(f"u_in{k}") for k in range(RG * G)]
        v_in = [sem(f"v_in{k}") for k in range(RG * G)]
        dots_done, gelu_done, diag_done, y_done = (sem(n) for n in ("dots_done", "gelu_done", "diag_done", "y_done"))
        var2, sd2, res_done = sem("var2"), sem("sd2"), sem("res_done")
        passed = {e: sem(f"passed_{e}") for e in ("pe", "act", "dve", "pool")}

        block = ctx.enter_context(nc.Block())

        @block.sync
        def _(sp):
            for q in range(4):
                sp.dma_start(kw[:, 4 * q:4 * q + 4, :], w_kw[:, 4 * q:4 * q + 4, :]).then_inc(kw_in[q], 16)
                sp.dma_start(x_raw[:, 4 * q:4 * q + 4, :], xT[:, 4 * q:4 * q + 4, :]).then_inc(x_in[q], 16)
            for k in range(RING):
                sp.dma_start(w_raw[k], w_stream[k]).then_inc(w_in[k], 16)
            with sp.Fori(1, U_END // RING) as r:
                for k in range(RING):
                    sp.wait_ge(w_used, r * RING + (k - RING + 1))
                    sp.dma_start(w_raw[k], w_stream[bass.ds(r * RING + k, 1)].rearrange("a p n -> (a p) n")).then_inc(w_in[k], 16)
            for i in range(TI):
                sp.wait_ge(res_done, i + 1)
                sp.dma_start(out[i * P:(i + 1) * P, :], x1[:, i, :]).then_inc(out_done, 16)
            sp.wait_ge(out_done, 16 * TI)

        @block.gpsimd
        def _(pool):
            pool.memset(ident[:, :], 0.0)
            pool.memset(ident_a[:, :], 0.0)
            pool.memset(flip[:, :], 0.0)
            pool.memset(mean_w[:, :], 1.0 / DC)
            pool.memset(ones_row[:, :], 1.0)
            pool.memset(eps[:, :], EPS)
            pool.iota(iota_i[:, :].rearrange("p (r j) -> p r j", j=TOP), [[0, TOP], [1, TOP]], channel_multiplier=0).then_inc(pool_const, 1)
            pool.wait_ge(pool_const, 1)
            pool.affine_select(out=ident[:, :], in_=ident[:, :], compare_op=ALU.not_equal, fill=1.0,
                               base=0, pattern=[[-1, P]], channel_multiplier=1)
            pool.affine_select(out=ident_a[:, :], in_=ident_a[:, :], compare_op=ALU.not_equal, fill=ALPHA,
                               base=0, pattern=[[-1, P]], channel_multiplier=1)
            pool.affine_select(out=flip[:, :], in_=flip[:, :], compare_op=ALU.not_equal, fill=1.0,
                               base=-(P - 1), pattern=[[1, P]], channel_multiplier=1).then_inc(pool_const, 1)
            def lower(n, u, k):
                pool.wait_ge(hi_done, u + 1)
                pool.tensor_tensor(w_lo[k], w_raw[k], w_hi[k].bitcast(F32), ALU.subtract).then_inc(lo_pool, 1)

            def cut(ready, ts, fill, n):
                for i in range(TI):
                    pool.wait_ge(ready, i + 1)
                    pool.affine_select(out=ts[i], in_=ts[i], compare_op=ALU.is_ge, fill=fill,
                                       base=i * P, pattern=[[-1, (i + 1) * P]], channel_multiplier=1).then_inc(causal, 1)

            for m in range(2):
                lower(m, U_GLU + m, m)
            cut(scored, acc, FILL, 0)
            for m in range(2, 4):
                lower(m, U_GLU + m, m)
            with pool.Fori(1, 4) as r:
                for k in range(RING):
                    lower(r * RING + k, r * RING + (U_GLU + k), k)
            cut(masked, mask, NEG, TI)
            with pool.Fori(0, (U_OUT - U_V) // RING) as r:
                for k in range(RING):
                    lower(r * RING + (16 + k), r * RING + (U_V + k), k)
            pool.wait_ge(w_used, U_OUT)
            pool.dma_start(b_row, b_out).then_inc(b_in, 16)
            pool.wait_ge(logit_read, CC)
            pool.dma_start(sub, w_sub).then_inc(sub_in, 16)
            pool.wait_ge(att_turned, 4)
            pool.dma_start(x1, x_tok.rearrange("(i p) d -> p i d", p=P)).then_inc(row_in, 16)
            for k in range(2):
                lower(40 + k, U_WQ + k, k)
            pool.wait_ge(w_used, U_WQ)
            for k in range(2):
                pool.dma_start(rows[:, k, :], ln_rows[k:k + 1, :].to_broadcast([P, D])).then_inc(row1_in, 16)
            for m in range(1, KC // 2, 2):
                pool.wait_ge(x1h_done, m + 1)
                pool.tensor_tensor(xl[:, 2 * m:2 * m + 2, :].rearrange("p c t -> p (c t)"), x1c[m % 4],
                                   xh[:, 2 * m:2 * m + 2, :].rearrange("p c t -> p (c t)").bitcast(F32),
                                   ALU.subtract).then_inc(x1T_odd, 1)
            for k in range(2, RING):
                lower(40 + k, U_WQ + k, k)
            with pool.Fori(1, 4) as r:
                for k in range(RING):
                    lower(r * RING + (40 + k), r * RING + (U_WQ + k), k)
            pool.wait_ge(x1_done, TI)
            for k in range(2):
                pool.dma_start(rows[:, k, :], ln_rows[k + 2:k + 3, :].to_broadcast([P, D])).then_inc(row2_in, 16)

            for i in range(TI):
                with pool.Fori(0, GROUPS // RG) as r:
                    for k in range(RG):
                        g = r * RG + (k + i * GROUPS)
                        if k == 0:
                            pool.wait_ge(picked, r + (i * GROUPS // RG + 1))
                        pool.wait_ge(dots_done, g + 1)
                        pool.wait_ge(y_done, g + 1)
                        pool.sem_inc(passed["pool"], 1)
                        pool.tensor_copy(eslot[k][:, :], eid[:, i, bass.ds((r * RG + k) * G, G)]).then_inc(eslot_done, 1)
                        pool.wait_ge(eslot_done, g + 1)
                        pool.sem_inc(passed["pool"], 1)
                        for tab, dst, land in ((u_tab, u_ring, u_in), (v_tab, v_ring, v_in)):
                            for j in range(G):
                                if k * G + j == 2:
                                    pool.wait_ge(w_used, U_END)
                                if k == RG - 1 and j == 0:
                                    pool.wait_ge(key_copied, 2 + 2 * PH)
                                pool.indirect_dma_start(
                                    dst[k * G + j], None, tab,
                                    bass.IndirectOffsetOnAxis(ap=eslot[k][:, j:j + 1], axis=0),
                                ).then_inc(land[k * G + j], 16)

        @block.tensor
        def _(pe):
            def unit_in(lo, n):
                pe.wait_ge(lo, n + 1)

            def exact(dst, a, b, first, last):
                pe.matmul(dst, a[0], b[0], start=first, stop=False)
                pe.matmul(dst, a[0], b[1], start=False, stop=False)
                return pe.matmul(dst, a[1], b[0], start=False, stop=last)

            def project(k, dst, lo, n, x1_arrives=False):
                unit_in(lo, n)
                w = [t[k].rearrange("p (c n) -> p c n", c=KC) for t in (w_hi, w_lo)]
                for c in range(KC):
                    if x1_arrives and c % 2 == 0:
                        pe.wait_ge(x1T_odd if c % 4 else x1T_even, c // 4 + 1)
                    last = exact(dst, [t[:, c, :] for t in w], [xh[:, c, :], xl[:, c, :]], c == 0, c == KC - 1)
                last.then_inc(w_used, 1)

            for c in range(KC):
                if c % 4 == 0:
                    pe.wait_ge(kw_in[c // 4], 16)
                    pe.wait_ge(x_in[c // 4], 16)
                pe.matmul(ps[0][:, 0:S], kw[:, c, 0:P], x_raw[:, c, :], start=c == 0, stop=c == KC - 1)
            for i in range(TI):
                for c in range(KC):
                    last = pe.matmul(ps[1][:, i * NH:(i + 1) * NH], x_raw[:, c, i * P:(i + 1) * P], kw[:, c, P:KWCOL],
                                     start=c == 0, stop=c == KC - 1)
            last.then_inc(kw_done, 1)
            pe.wait_ge(small_in, 16 * 6)
            pe.matmul(ps[7][0:NH, 0:SKEW], relb[:, :], onehot[:, :], start=True, stop=True).then_inc(row_done, 1)
            pe.wait_ge(kw_copied, 2)
            pe.wait_ge(x_split, 4)

            def index_scores(u, k):
                pe.wait_ge(qidx_copied, u + 3)
                pe.wait_ge(relu_done, u + 1)
                for i in range(TI):
                    for j in range(2):
                        n = (i + 1) * P
                        last = pe.matmul(ps[2 + 2 * j + k % 2][:, span(i)],
                                         qidx[k % 2][j * HD:(j + 1) * HD, i * P:(i + 1) * P],
                                         kidxT[j * HD:(j + 1) * HD, 0:n], start=True, stop=True)
                last.then_inc(score_done, 1)

            with pe.Fori(0, CC // RING) as r:
                for k in range(RING):
                    u = r * RING + k
                    pe.wait_ge(qidx_copied, u + 1)
                    project(k, ps[k % 2][:, 0:S], lo_dve, u)
                    if k:
                        index_scores(u - 1, k - 1)
                index_scores(r * RING + (RING - 1), RING - 1)

            pe.wait_ge(skew_in, 16)
            pe.wait_ge(pool_const, 2)
            for n in range(8):
                pe.wait_ge(bias_copied, max(n - 1, 0))
                pe.matmul(ps[6 + n % 2][:, :], flip[:, :], skew[:, 2 * n:2 * n + 2, :].rearrange("p h s -> p (h s)"),
                          start=True, stop=True).then_inc(flip_done, 1)

            pe.wait_ge(relu_done, CC + 2)
            with pe.Fori(0, CC // 4) as r:
                for k in range(4):
                    pe.wait_ge(glu_done, r * 4 + (k + 1))
                    if k == 3:
                        pe.wait_ge(bias_copied, 8)
                    for half in range(2):
                        s = 2 * k + half
                        project(s % RING, ps[s][:, 0:S], lo_pool, r * 8 + s)

            for n in range(2):
                pe.wait_ge(glu_done, 4 + CC // 2 + 1 + n)
                for q in range(RING):
                    unit_in(lo_pool, 16 + n * RING + q)
                    w = [t[q].rearrange("p (c n) -> p c n", c=4) for t in (w_hi, w_lo)]
                    for c in range(4):
                        for i in range(TI):
                            last = exact(ps[2 * n + i], [t[:, 4 * q + c, i * P:(i + 1) * P] for t in (xh, xl)],
                                         [t[:, c, :] for t in w], q + c == 0, q + c == 6)
                    last.then_inc(w_used, 1)

            def qk(hp, k):
                pe.wait_ge(qk_copied, hp * 2)
                project(2 * k, ps[0][:, 0:S], lo_pool, hp * 2 + 24)
                project(2 * k + 1, ps[1][:, 0:S], lo_pool, hp * 2 + 25)

            def logits(hp):
                pe.wait_ge(qk_copied, hp * 2 + 2)
                pe.wait_ge(logit_read, hp)
                for i in range(TI):
                    n = (i + 1) * P
                    for j in range(2):
                        last = pe.matmul(ps[2 + j][:, span(i)], qT[j * HD:(j + 1) * HD, i * P:(i + 1) * P],
                                         kT[j * HD:(j + 1) * HD, 0:n], start=True, stop=True)
                last.then_inc(logit_done, 1)

            def turn(hp):
                pe.wait_ge(exp_done, hp * 4 + 4)
                for i in range(TI):
                    for j in range(2):
                        for b in range(i + 1):
                            last = pe.transpose(ps[4 + i][:, (j * (i + 1) + b) * P:(j * (i + 1) + b + 1) * P],
                                                lg[i][:, j, b * P:(b + 1) * P], ident[:, :])
                last.then_inc(turned, 1)

            def values(hp):
                pe.wait_ge(pt_copied, hp * 2 + 2)
                pe.wait_ge(att_done, hp + 1)
                for i in range(TI):
                    for j in range(2):
                        for b in range(i + 1):
                            last = pe.matmul(ps[6][:, (2 * i + j) * HD:(2 * i + j + 1) * HD],
                                             pT[i][:, (j * (i + 1) + b) * P:(j * (i + 1) + b + 1) * P],
                                             v_sb[:, b, bass.ds(hp * P + j * HD, HD)], start=b == 0, stop=b == i)
                last.then_inc(pv_done, 1)

            pe.wait_ge(v_copied, 2)
            project(0, ps[0][:, 0:S], lo_pool, 24)
            pe.wait_ge(conv_done, CC)
            for c in range(CC):
                last = pe.matmul(ps[7][:, 0:S], mean_w[:, :], convT[:, c, :], start=c == 0, stop=c == CC - 1)
            last.then_inc(mean_done, 1)
            project(1, ps[1][:, 0:S], lo_pool, 25)
            pe.wait_ge(squared, 1)
            for c in range(CC):
                last = pe.matmul(ps[7][:, 0:S], mean_w[:, :], sq[:, c, :], start=c == 0, stop=c == CC - 1)
            last.then_inc(var_done, 1)
            pe.wait_ge(v_copied, 4)
            logits(0)
            with pe.Fori(0, 3) as r:
                for k in range(2):
                    hp = r * 2 + (k + 1)
                    qk(hp, 1 - k)
                    turn(hp - 1)
                    logits(hp)
                    values(hp - 1)
            qk(7, 1)
            turn(6)
            logits(7)
            values(6)

            def mix(n, q, chunks):
                bank = 6 if n % 2 else 0
                unit_in(lo_dve, 8 + n * RING + q)
                w = [t[q].rearrange("p (c n) -> p c n", c=4) for t in (w_hi, w_lo)]
                for c in chunks:
                    for i in range(TI):
                        last = exact(ps[bank + i], [t[:, 4 * q + c, i * P:(i + 1) * P] for t in (cat_h, cat_l)],
                                     [t[:, c, :] for t in w], q + c == 0, False)
                if chunks[-1] == 3:
                    last.then_inc(w_used, 1)

            pe.wait_ge(qk_copied, 2 * CC)
            pe.wait_ge(cat_lo, CC)
            mix(0, 0, range(4))
            turn(7)
            mix(0, 1, range(2))
            values(7)
            mix(0, 1, range(2, 4))

            pe.wait_ge(att_done, CC + 1)
            for m in range(4):
                for c in range(2):
                    for i in range(TI):
                        last = pe.transpose(ps[2 + m][:, (2 * c + i) * P:(2 * c + i + 1) * P],
                                            att[:, i, (2 * m + c) * P:(2 * m + c + 1) * P], ident[:, :])
                last.then_inc(att_turned, 1)

            for n in range(4):
                bank = 6 if n % 2 else 0
                pe.wait_ge(mix_read, max(n - 1, 0) * TI)
                for q in range(RING) if n else (2, 3):
                    if n == 0:
                        pe.wait_ge(att_lo, 2 * (q - 1))
                    mix(n, q, range(4))
                pe.wait_ge(b_in, 16)
                for i in range(TI):
                    last = pe.matmul(ps[bank + i], ones_row[:, :], b_row[:, n * 512:(n + 1) * 512], start=False, stop=True)
                last.then_inc(mix_done, 1)

            for m in range(KC // 2):
                pe.wait_ge(xn0_done, m // 2 + 1)
                pe.wait_ge(xn1_done, m // 2 + 1)
                pe.wait_ge(x1c_done, max(m - 3, 0))
                for c in range(2):
                    for i in range(TI):
                        last = pe.transpose(ps[2 + m % 4][:, (2 * c + i) * P:(2 * c + i + 1) * P],
                                            x1[:, i, (2 * m + c) * P:(2 * m + c + 1) * P], ident[:, :])
                last.then_inc(xn_turned, 1)

            def key_scores(u, k):
                pe.wait_ge(qc_copied, u + 3)
                pe.wait_ge(key_copied, u + 1)
                for i in range(TI):
                    last = pe.matmul(ps[2 + k % 2][:, i * PK:(i + 1) * PK], qc[k % 2][:, i * P:(i + 1) * P],
                                     sub[:, bass.ds(u * PK, PK)], start=True, stop=True)
                last.then_inc(key_done, 1)

            pe.wait_ge(mix_read, 8)
            pe.wait_ge(sub_in, 16)
            with pe.Fori(0, 2 * PH // RING) as r:
                for k in range(RING):
                    u = r * RING + k
                    pe.wait_ge(qc_copied, u + 1)
                    project(k, ps[k % 2][:, 0:S], lo_pool, u + 40, k == 0)
                    if k:
                        key_scores(u - 1, k - 1)
                key_scores(r * RING + (RING - 1), RING - 1)

            for i in range(TI):
                pe.wait_ge(x1_done, i + 1)
                if i == 0:
                    pe.wait_ge(key_copied, 2 * PH + 2)
                for n in range(4):
                    pe.matmul(ps[4 * i + n][:, :], ident_a[:, :], x1[:, i, n * 512:(n + 1) * 512], start=True, stop=False,
                              skip_group_check=True)
                with pe.Fori(0, GROUPS // RG) as r:
                    for k in range(RG):
                        g = r * RG + (k + i * GROUPS)
                        pe.wait_ge(diag_done, g + 1)
                        for j in range(G):
                            pe.wait_ge(v_in[k * G + j], r * 16 + (16 + 16 * i * GROUPS // RG))
                            for n in range(4):
                                last = pe.matmul(ps[4 * i + n][:, :], diag[k][:, j, :], v_ring[k * G + j][:, n * 512:(n + 1) * 512],
                                                 start=False, stop=True, skip_group_check=True)
                        last.then_inc(y_done, 1)

        @block.scalar
        def _(act):
            act.dma_start(relb[:, :], rel_bias).then_inc(small_in, 16)
            act.dma_start(onehot[:, :], bucket1h).then_inc(small_in, 16)
            act.dma_start(conv_sb[:, :], conv_p).then_inc(small_in, 16)
            act.dma_start(cln_sb[:, :], cln).then_inc(small_in, 16)
            act.dma_start(ln1c[:, 0:KC], ln1_col[0]).then_inc(small_in, 16)
            act.dma_start(ln1c[:, KC:2 * KC], ln1_col[1]).then_inc(small_in, 16)
            act.sem_inc(qidx_copied, 2)
            act.sem_inc(relu_done, 2)
            act.sem_inc(qc_copied, 2)
            act.sem_inc(key_copied, 2)

            def upper(u, k):
                act.wait_ge(w_in[k], (u - k) * (16 // RING) + 16)
                if not isinstance(u, int) or u >= RING:
                    act.wait_ge(w_used, u - (RING - 1))
                    if not isinstance(u, int):
                        act.sem_inc(passed["act"], 1)
                act.activation(w_hi[k], w_raw[k], ACT.Copy).then_inc(hi_done, 1)

            for q in range(4):
                act.wait_ge(x_in[q], 16)
                act.activation(xh[:, 4 * q:4 * q + 4, :], x_raw[:, 4 * q:4 * q + 4, :], ACT.Copy).then_inc(x_hi_done, 1)
            upper(0, 0)
            upper(1, 1)
            act.wait_ge(kw_done, 1)
            act.activation(kidxT[:, :], ps[0][:, 0:S], ACT.Copy).then_inc(kw_copied, 1)
            act.activation(widx[:, :], ps[1][:, 0:TI * NH], ACT.Copy).then_inc(kw_copied, 1)

            def relu(u):
                b = u % 2
                act.wait_ge(score_done, u + 1)
                if u >= 2:
                    act.wait_ge(idx_added, u - 1)
                for j in range(2):
                    last = act.activation(rel[b][:, j, :], ps[2 + 2 * j + b][:, 0:S + P], ACT.Relu)
                last.then_inc(relu_done, 1)

            act.wait_ge(row_done, 1)
            act.activation(dist_row[:, :], ps[7][0:NH, 0:SKEW], ACT.Copy).then_inc(row_copied, 1)
            act.wait_ge(row_copied, 1)
            act.dma_start(row_scratch, dist_row[:, :]).then_inc(row_out, 16)

            for u in range(CC):
                upper(u + 2, (u + 2) % RING)
                if u == 2:
                    act.wait_ge(row_out, 16)
                    act.dma_start(skew, bass.AP(tensor=row_scratch.tensor, offset=0, ap=[[1, P], [SKEW, NH], [1, S]])).then_inc(skew_in, 16)
                act.wait_ge(w_used, U_IDX + u + 1)
                if u >= 2:
                    act.wait_ge(score_done, u - 1)
                act.activation(qidx[u % 2][:, :], ps[u % 2][:, 0:S], ACT.Copy).then_inc(qidx_copied, 1)
                if u % RING:
                    relu(u - 1)
                if u % RING == RING - 1:
                    relu(u)

            for n in range(8):
                act.wait_ge(flip_done, n + 1)
                act.activation(bias[:, 2 * n:2 * n + 2, :].rearrange("p h s -> p (h s)"), ps[6 + n % 2][:, :], ACT.Copy).then_inc(bias_copied, 1)

            for c in range(CC):
                upper(U_GLU + 2 * c + 2, (2 * c + 2) % RING)
                upper(U_GLU + 2 * c + 3, (2 * c + 3) % RING)
                act.wait_ge(w_used, U_GLU + 2 * c + 2)
                if c >= 4:
                    act.wait_ge(glu_done, 4 + c - 3)
                act.activation(sig[c % 4][:, :], ps[2 * (c % 4) + 1][:, 0:S], ACT.Sigmoid).then_inc(sig_done, 1)

            for n in range(2):
                for q in range(RING):
                    upper(U_V + RING * n + 2 + q, (2 + q) % RING)
                act.wait_ge(w_used, U_V + RING * (n + 1))
                for i in range(TI):
                    act.activation(v_sb[:, i, n * 512:(n + 1) * 512], ps[2 * n + i][:, :], ACT.Copy).then_inc(v_copied, 1)

            act.wait_ge(centred, 1)
            act.activation(sq.rearrange("p c t -> p (c t)"), convT.rearrange("p c t -> p (c t)"), ACT.Square).then_inc(squared, 1)

            def qk_copy(hp, k):
                upper(hp * 2 + (U_QK + 2), (2 * k + 2) % RING)
                upper(hp * 2 + (U_QK + 3), (2 * k + 3) % RING)
                act.wait_ge(w_used, hp * 2 + (U_QK + 1))
                act.wait_ge(logit_done, hp)
                act.activation(qT[:, :], ps[0][:, 0:S], ACT.Copy, scale=HD ** -0.5).then_inc(qk_copied, 1)
                act.wait_ge(w_used, hp * 2 + (U_QK + 2))
                act.activation(kT[:, :], ps[1][:, 0:S], ACT.Copy).then_inc(qk_copied, 1)

            def exps(hp, b):
                act.wait_ge(max_done, hp + 1)
                for i in range(TI):
                    for j in range(2):
                        a = 2 * i + j
                        act.activation(lg[i][:, j, :], lg[i][:, j, :], ACT.Exp, bias=nm[:, a:a + 1],
                                       accum_out=rsum[b][:, a:a + 1]).then_inc(exp_done, 1)

            def pt_copy(hp):
                act.wait_ge(turned, hp + 1)
                act.wait_ge(pv_done, hp + 1)
                act.activation(pT[0][:, :], ps[4][:, 0:2 * P], ACT.Copy).then_inc(pt_copied, 1)
                act.activation(pT[1][:, :], ps[5][:, :], ACT.Copy).then_inc(pt_copied, 1)

            qk_copy(0, 0)
            act.wait_ge(var_done, 1)
            act.activation(rstd_c[:, :], ps[7][:, 0:S], ACT.Sqrt, bias=eps[:, :]).then_inc(sd_done, 1)
            act.wait_ge(normed, 1)
            for c in range(CC):
                act.activation(convT[:, c, :], convT[:, c, :], ACT.Silu, scale=cln_sb[:, c:c + 1],
                               bias=cln_sb[:, CC + c:CC + c + 1]).then_inc(conv_out, 1)
            exps(0, 0)
            act.wait_ge(conv_out, CC)
            act.activation(cat_h[:, 0:CC, :], convT, ACT.Copy).then_inc(conv_out, 1)
            with act.Fori(0, 3) as r:
                for k in range(2):
                    hp = r * 2 + (k + 1)
                    qk_copy(hp, 1 - k)
                    pt_copy(hp - 1)
                    exps(hp, 1 - k)
            qk_copy(7, 1)
            pt_copy(6)
            exps(7, 1)
            upper(U_OUT + 2, 2)
            pt_copy(7)
            upper(U_OUT + 3, 3)

            for m in range(4):
                act.wait_ge(att_turned, m + 1)
                act.activation(cat_h[:, CC + 2 * m:CC + 2 * m + 2, :].rearrange("p c t -> p (c t)"), ps[2 + m], ACT.Copy).then_inc(att_copied, 1)
            for u in range(U_OUT + RING, U_WQ + 2):
                upper(u, u % RING)

            act.wait_ge(var1, 1)
            act.activation(sd[:, :], mv[:, :, 1], ACT.Sqrt, bias=eps[:, :]).then_inc(sd1, 1)
            act.wait_ge(shift1, 1)
            for n in range(4):
                x_n = x1[:, 1, n * 512:(n + 1) * 512]
                act.activation(x_n, x_n, ACT.Identity, scale=rstd[:, 1:2], bias=nmr[:, 1:2]).then_inc(xn1_done, 1)
            for m in range(KC // 2):
                act.wait_ge(x1c_done, m + 1)
                act.activation(xh[:, 2 * m:2 * m + 2, :].rearrange("p c t -> p (c t)"), x1c[m % 4], ACT.Copy).then_inc(x1h_done, 1)

            def key_copy(u):
                act.wait_ge(key_done, u + 1)
                if u >= 4:
                    act.wait_ge(key_used, u // 2 - 1)
                act.activation(sw[u % 4], ps[2 + u % 2][:, 0:PK], ACT.Copy)
                act.activation(later[:, u * PK:(u + 1) * PK], ps[2 + u % 2][:, PK:2 * PK], ACT.Copy).then_inc(key_copied, 1)

            for u in range(2 * PH):
                if U_WQ + u + 2 < U_END:
                    upper(U_WQ + u + 2, (u + 2) % RING)
                act.wait_ge(w_used, U_WQ + u + 1)
                if u >= 2:
                    act.wait_ge(key_done, u - 1)
                act.activation(qc[u % 2][:, :], ps[u % 2][:, 0:S], ACT.Copy).then_inc(qc_copied, 1)
                if u % RING:
                    key_copy(u - 1)
                if u % RING == RING - 1:
                    key_copy(u)

            def gate_exps(i):
                act.wait_ge(gate_sub, i + 1)
                act.activation(gate[:, i, :], gate[:, i, :], ACT.Exp).then_inc(gate_exp, 1)

            def gelus(first, last, i):
                with act.Fori(first, last) as r:
                    for k in range(RG):
                        act.wait_ge(dots_done, r * RG + (k + i * GROUPS + 1 + RG))
                        act.activation(gel[k][:, :], dots[k][:, :], ACT.Gelu).then_inc(gelu_done, 1)

            def sd_rows(i):
                act.wait_ge(var2, i + 1)
                act.activation(sd[:, i:i + 1], mv[:, i, 1:2], ACT.Sqrt, bias=eps[:, :]).then_inc(sd2, 1)

            gate_exps(0)
            gelus(0, GROUPS // RG, 0)
            gate_exps(1)
            gelus(0, 2, 1)
            sd_rows(0)
            gelus(2, GROUPS // RG, 1)
            sd_rows(1)

        @block.vector
        def _(dve):
            steps = [0]

            def link(ins):
                steps[0] += 1
                ins.then_inc(dve_step, 1)
                dve.wait_ge(dve_step, steps[0])

            dve.sem_inc(glu_done, 4)
            dve.sem_inc(dots_done, RG)
            dve.sem_inc(y_done, RG)
            dve.sem_inc(att_done, 1)
            dve.sem_inc(pv_done, 1)
            dve.memset(cbuf[:, :], 0.0)
            for i in range(TI):
                dve.memset(acc[i][:, :], 0.0)
            dve.wait_ge(pool_const, 1)
            link(dve.tensor_copy(iota_f[:, :], iota_i[:, :]))

            def lower(u):
                k = u % RING
                dve.wait_ge(hi_done, u + 1)
                dve.tensor_tensor(w_lo[k], w_raw[k], w_hi[k].bitcast(F32), ALU.subtract).then_inc(lo_dve, 1)

            for q in range(4):
                dve.wait_ge(x_hi_done, q + 1)
                dve.tensor_tensor(xl[:, 4 * q:4 * q + 4, :], x_raw[:, 4 * q:4 * q + 4, :], xh[:, 4 * q:4 * q + 4, :].bitcast(F32),
                                  ALU.subtract).then_inc(x_split, 1)
            lower(0)
            lower(1)

            dve.wait_ge(kw_copied, 2)
            for u in range(CC):
                if u + 2 < CC:
                    lower(u + 2)
                dve.wait_ge(relu_done, 2 + u + 1)
                for j in range(2):
                    for i in range(TI):
                        h = i * NH + 2 * u + j
                        last = dve.scalar_tensor_tensor(out=acc[i][:, :], in0=rel[u % 2][:, j, span(i)], scalar=widx[:, h:h + 1],
                                                        in1=acc[i][:, :], op0=ALU.mult, op1=ALU.add)
                    if j == 0:
                        link(last)
                last.then_inc(idx_added, 1)
                dve.wait_ge(idx_added, u + 1)
            for i in range(TI):
                dve.sem_inc(scored, 1)
            dve.wait_ge(causal, TI)
            a, b = acc, acc_b
            for n in range(NSEL // 8):
                for i in range(TI):
                    last = dve.max(best8[i][:, :], a[i][:, :])
                link(last)
                for i in range(TI):
                    last = dve.match_replace(b[i][:, :], best8[i][:, :], a[i][:, :], TAKEN)
                link(last)
                a, b = b, a
            for i in range(TI):
                dve.tensor_scalar(mask[i][:, :], a[i][:, :], TAKEN / 2, NEG, ALU.is_gt, ALU.mult).then_inc(masked, 1)

            dve.wait_ge(small_in, 16 * 6)
            for c in range(CC):
                dve.wait_ge(sig_done, c + 1)
                dve.tensor_copy(conv_c[:, :], conv_sb[:, c * (TAPS + 1):(c + 1) * (TAPS + 1)])
                dve.tensor_tensor(cbuf[:, TAPS - 1:], ps[2 * (c % 4)][:, 0:S], sig[c % 4][:, :], ALU.mult).then_inc(glu_done, 1)
                dve.wait_ge(glu_done, 4 + c + 1)
                dve.tensor_scalar(cacc[0], cbuf[:, 0:S], conv_c[:, 0:1], conv_c[:, TAPS:TAPS + 1], ALU.mult, ALU.add)
                link(dve.tensor_scalar(cacc[1], cbuf[:, 1:S + 1], conv_c[:, 1:2], None, ALU.mult))
                for t in range(2, TAPS):
                    last = dve.scalar_tensor_tensor(out=cacc[t % 2], in0=cbuf[:, t:t + S], scalar=conv_c[:, t:t + 1],
                                                    in1=cacc[t % 2], op0=ALU.mult, op1=ALU.add)
                    if t % 2 or t == TAPS - 1:
                        link(last)
                dve.tensor_tensor(convT[:, c, :], cacc[0], cacc[1], ALU.add).then_inc(conv_done, 1)
                dve.wait_ge(conv_done, c + 1)

            dve.wait_ge(mean_done, 1)
            for c in range(CC):
                last = dve.tensor_tensor(convT[:, c, :], convT[:, c, :], ps[7][:, 0:S], ALU.subtract)
            last.then_inc(centred, 1)

            def softmax_in(hp):
                dve.wait_ge(logit_done, hp + 1)
                for i in range(TI):
                    last = dve.tensor_tensor(lg[i][:, :, :], psum[:, 2:4, span(i)],
                                             bias[:, 2 * hp:2 * hp + 2, P - i * P:S], ALU.add)
                last.then_inc(logit_read, 1)
                dve.wait_ge(logit_read, hp + 1)
                for i in range(TI):
                    for j in range(2):
                        last = dve.tensor_tensor_reduce(lg[i][:, j, :], lg[i][:, j, :], mask[i][:, :], 1.0, -3.4e38,
                                                        ALU.add, ALU.max, mx[:, 2 * i + j:2 * i + j + 1])
                link(last)
                dve.tensor_scalar(nm[:, :], mx[:, :], -1.0, None, ALU.mult).then_inc(max_done, 1)

            def heads_out(hp):
                dve.wait_ge(pv_done, hp + 2)
                link(dve.reciprocal(rinv[:, :], rsum[hp % 2][:, :]))
                dve.tensor_tensor(att[:, :, hp * P:(hp + 1) * P].rearrange("p i (j d) -> p i j d", j=2),
                                  ps[6][:, 0:4 * HD].rearrange("p (i j d) -> p i j d", i=2, j=2),
                                  rinv[:, :].rearrange("p (i j o) -> p i j o", i=2, o=1).to_broadcast([P, 2, 2, HD]),
                                  ALU.mult).then_inc(att_done, 1)

            dve.wait_ge(sd_done, 1)
            link(dve.reciprocal(cacc[0], rstd_c[:, :]))
            dve.wait_ge(squared, 1)
            for c in range(CC):
                last = dve.tensor_tensor(convT[:, c, :], convT[:, c, :], cacc[0], ALU.mult)
            last.then_inc(normed, 1)
            dve.wait_ge(bias_copied, 8)
            dve.wait_ge(causal, 2 * TI)
            softmax_in(0)
            dve.wait_ge(conv_out, CC + 1)
            dve.tensor_tensor(cat_l[:, 0:CC, :], convT, cat_h[:, 0:CC, :].bitcast(F32), ALU.subtract).then_inc(cat_lo, CC)
            for hp in range(1, CC):
                if hp == CC - 1:
                    lower(U_OUT)
                softmax_in(hp)
                if hp == CC - 1:
                    lower(U_OUT + 1)
                heads_out(hp - 1)
            heads_out(CC - 1)
            lower(U_OUT + 2)
            for m in range(4):
                dve.wait_ge(att_copied, m + 1)
                if m == 0:
                    dve.wait_ge(cat_lo, CC)
                c0 = CC + 2 * m
                dve.tensor_tensor(cat_l[:, c0:c0 + 2, :].rearrange("p c t -> p (c t)"), ps[2 + m],
                                  cat_h[:, c0:c0 + 2, :].rearrange("p c t -> p (c t)").bitcast(F32), ALU.subtract).then_inc(att_lo, 1)

            for n in range(4):
                for q in range(RING):
                    if 2 < RING * n + q + 2 < U_WQ - U_OUT:
                        lower(U_OUT + RING * n + q + 2)
                if n == 0:
                    dve.wait_ge(row_in, 16)
                dve.wait_ge(mix_done, n + 1)
                for i in range(TI):
                    x_n = x1[:, i, n * 512:(n + 1) * 512]
                    dve.scalar_tensor_tensor(out=x_n, in0=x_n, scalar=ALPHA, in1=ps[(6 if n % 2 else 0) + i][:, :],
                                             op0=ALU.mult, op1=ALU.add).then_inc(mix_read, 1)
                dve.wait_ge(mix_read, TI * (n + 1))
                for i in range(TI):
                    last = dve.bn_stats(stats[:, 4 * i + n, :], x1[:, i, n * 512:(n + 1) * 512])
            link(last)
            for i in range(TI):
                last = dve.bn_aggr(mv[:, i, :], stats[:, 4 * i:4 * i + 4, :])
            last.then_inc(var1, 1)
            dve.wait_ge(sd1, 1)
            link(dve.reciprocal(rstd[:, :], sd[:, :]))
            dve.scalar_tensor_tensor(out=nmr[:, :], in0=mv[:, :, 0], scalar=-1.0, in1=rstd[:, :],
                                     op0=ALU.mult, op1=ALU.mult).then_inc(shift1, 1)
            for n in range(4):
                x_n = x1[:, 0, n * 512:(n + 1) * 512]
                dve.tensor_scalar(x_n, x_n, mv[:, 0, 0:1], rstd[:, 0:1], ALU.subtract, ALU.mult).then_inc(xn0_done, 1)

            def x1_lower(m):
                dve.wait_ge(x1h_done, m + 1)
                dve.tensor_tensor(xl[:, 2 * m:2 * m + 2, :].rearrange("p c t -> p (c t)"), x1c[m % 4],
                                  xh[:, 2 * m:2 * m + 2, :].rearrange("p c t -> p (c t)").bitcast(F32),
                                  ALU.subtract).then_inc(x1T_even, 1)

            for m in range(KC // 2):
                dve.wait_ge(xn_turned, m + 1)
                if m % 2 and m > 4:
                    dve.wait_ge(x1T_odd, (m - 3) // 2)
                for c in range(2):
                    kc = 2 * m + c
                    last = dve.tensor_scalar(x1c[m % 4][:, c * S:(c + 1) * S], ps[2 + m % 4][:, c * S:(c + 1) * S],
                                             ln1c[:, kc:kc + 1], ln1c[:, KC + kc:KC + kc + 1], ALU.mult, ALU.add)
                last.then_inc(x1c_done, 1)
                if m % 2:
                    x1_lower(m - 1)
            dve.wait_ge(xn0_done, 4)
            dve.wait_ge(xn1_done, 4)
            dve.wait_ge(row1_in, 32)
            for i in range(TI):
                last = dve.tensor_tensor(x1[:, i, :], x1[:, i, :], rows[:, 0, :], ALU.mult)
            link(last)
            for i in range(TI):
                dve.tensor_tensor(x1[:, i, :], x1[:, i, :], rows[:, 1, :], ALU.add).then_inc(x1_done, 1)

            def top16(jobs):
                for v, _, src, _ in jobs:
                    last = dve.max(v[:, 0:8], src)
                link(last)
                for v, ids, src, buf in jobs:
                    dve.max_index(ids[:, 0:8], v[:, 0:8], src)
                    last = dve.match_replace(buf, v[:, 0:8], src, TAKEN)
                link(last)
                for v, _, _, buf in jobs:
                    last = dve.max(v[:, 8:16], buf)
                link(last)
                for v, ids, _, buf in jobs:
                    last = dve.max_index(ids[:, 8:16], v[:, 8:16], buf)
                return last

            square = [P, TOP, TOP]
            iota_v = iota_f[:, :].rearrange("p (r j) -> p r j", j=TOP)

            def across(t):
                return t.rearrange("p (r o) -> p r o", o=1).to_broadcast(square)

            def down(t):
                return t.rearrange("p (o j) -> p o j", o=1).to_broadcast(square)

            def retrieve(i, h, halves):
                last = top16([(val[c][:, :], idx[c][:, :], halves[c], sw2[c]) for c in range(2)])
                last.then_inc(key_used, 1)
                dve.wait_ge(key_used, i * PH + h + 1)
                link(dve.tensor_tensor(cand.rearrange("p (a b) -> p a b", a=TOP), across(val[0][:, :]), down(val[1][:, :]), ALU.add))
                link(top16([(gate[:, i, h * TOP:(h + 1) * TOP], pos[:, :], cand, cand2)]))
                dve.tensor_scalar(posp[0][:, :], pos[:, :], 4, None, ALU.logical_shift_right)
                dve.tensor_scalar(posp[1][:, :], pos[:, :], TOP - 1, None, ALU.bitwise_and)
                for c in range(2):
                    last = dve.tensor_copy(idxf[c][:, :], idx[c][:, :])
                link(last)
                for c in range(2):
                    last = dve.tensor_copy(posf[c][:, :], posp[c][:, :])
                link(last)
                for c in range(2):
                    last = dve.tensor_tensor(hit[c], across(posf[c][:, :]), iota_v, ALU.is_equal)
                link(last)
                for c in range(2):
                    last = dve.tensor_tensor(hit[c], hit[c], down(idxf[c][:, :]), ALU.mult)
                link(last)
                for c in range(2):
                    last = dve.tensor_reduce(pick[c][:, :], hit[c], AX.X, ALU.add)
                link(last)
                link(dve.scalar_tensor_tensor(out=eid[:, i, h * TOP:(h + 1) * TOP], in0=pick[0][:, :], scalar=float(PK),
                                              in1=pick[1][:, :], op0=ALU.mult, op1=ALU.add))
                dve.sem_inc(picked, GROUPS // RG // PH)

            def gates(i):
                g = gate[:, i, :].rearrange("p (h r) -> p h r", h=PH)
                wide = [P, PH, TOP]
                link(dve.tensor_copy(gsum[:, :], g[:, :, 0]))
                dve.tensor_tensor(g, g, gsum[:, :].rearrange("p (a o) -> p a o", o=1).to_broadcast(wide), ALU.subtract).then_inc(gate_sub, 1)
                dve.wait_ge(gate_exp, i + 1)
                link(dve.tensor_reduce(gsum[:, :], g, AX.X, ALU.add))
                link(dve.reciprocal(ginv[:, :], gsum[:, :]))
                link(dve.tensor_tensor(g, g, ginv[:, :].rearrange("p (a o) -> p a o", o=1).to_broadcast(wide), ALU.mult))

            for h in range(PH):
                dve.wait_ge(key_copied, 2 + 2 * h + 2)
                retrieve(0, h, [sw[(2 * h + c) % 4] for c in range(2)])
            gates(0)

            def experts(first, last, i):
                with dve.Fori(first, last) as r:
                    for k in range(RG):
                        g = r * RG + (k + i * GROUPS)
                        for j in range(G):
                            s = k * G + j
                            dve.wait_ge(u_in[s], r * 16 + (16 + 16 * i * GROUPS // RG))
                            ins = dve.tensor_tensor_reduce(u_ring[s], u_ring[s], x1[:, i, :], 1.0, 0.0,
                                                           ALU.mult, ALU.add, dots[k][:, j:j + 1])
                        ins.then_inc(dots_done, 1)
                        dve.wait_ge(gelu_done, g + 1)
                        dve.wait_ge(y_done, g + 1)
                        for j in range(G):
                            ins = dve.tensor_scalar(diag[k][:, j, :], ident[:, :], gel[k][:, j:j + 1],
                                                    gate[:, i, bass.ds((r * RG + k) * G + j, 1)], ALU.mult, ALU.mult)
                        ins.then_inc(diag_done, 1)

            def norm_out(i):
                dve.wait_ge(y_done, RG + GROUPS * (i + 1))
                for n in range(4):
                    last = dve.bn_stats(stats[:, n, :], ps[4 * i + n][:, :])
                link(last)
                dve.bn_aggr(mv[:, i, :], stats[:, 0:4, :]).then_inc(var2, 1)
                dve.wait_ge(sd2, i + 1)
                link(dve.reciprocal(rstd[:, i:i + 1], sd[:, i:i + 1]))
                res = x1[:, i, :]
                dve.wait_ge(row2_in, 32)
                for n in range(4):
                    last = dve.tensor_scalar(res[:, n * 512:(n + 1) * 512], ps[4 * i + n][:, :], mv[:, i, 0:1], rstd[:, i:i + 1],
                                             ALU.subtract, ALU.mult)
                link(last)
                link(dve.tensor_tensor(res, res, rows[:, 0, :], ALU.mult))
                dve.tensor_tensor(res, res, rows[:, 1, :], ALU.add).then_inc(res_done, 1)

            per = GROUPS // RG // PH
            for h in range(PH):
                experts(h * per, (h + 1) * per, 0)
                for h1 in ([h] if h < PH - 2 else [PH - 2, PH - 1] if h == PH - 2 else []):
                    retrieve(1, h1, [later[:, (2 * h1 + c) * PK:(2 * h1 + c + 1) * PK] for c in range(2)])
            gates(1)
            experts(0, 2, 1)
            norm_out(0)
            experts(2, GROUPS // RG, 1)
            norm_out(1)


def _bucket_onehot():
    half = BUCKETS // 2
    d = np.maximum(S - 1 - np.arange(SKEW), 0)
    large = half + (np.log(np.maximum(d, 1).astype(np.float32) / np.float32(half))
                    / np.float32(np.log(MAX_DIST / half)) * np.float32(BUCKETS - half)).astype(np.int32)
    b = np.where(d < half, d, np.minimum(large, BUCKETS - 1))
    return (np.arange(BUCKETS)[:, None] == b[None, :]).astype(np.float32)


def kernel(x, w_in, w_out, b_out, dw_w, dw_b, conv_ln_g, conv_ln_b, rel_bias,
           ln1_g, ln1_b, peer_wq, peer_sub_keys, peer_u, peer_v, ln2_g, ln2_b):
    import concourse.bacc as _bacc
    from concourse.bass_utils import run_bass_kernel_spmd as _run

    def tiles(w):
        return np.asarray(w).reshape(KC, P, -1, P).transpose(2, 1, 0, 3).reshape(-1, P, UNIT)

    def strips(w):
        return np.asarray(w).reshape(4, 4, P, -1, 512).transpose(3, 0, 2, 1, 4).reshape(-1, P, UNIT)

    def pair(a, b):
        return np.stack([tiles(a), tiles(b)], 1).reshape(-1, P, UNIT)

    def cols(v, n):
        return np.asarray(v).reshape(n, P).T

    w = np.asarray(w_in)[0]
    c_q, c_k, c_v, c_qi, c_ki, c_wi = 2 * DC, 3 * DC, 4 * DC, 5 * DC, 6 * DC, 6 * DC + HD
    stream = np.concatenate([tiles(w[:, c_qi:c_ki]), pair(w[:, 0:DC], w[:, DC:2 * DC]), strips(w[:, c_v:c_qi]),
                             pair(w[:, c_q:c_k], w[:, c_k:c_v]), strips(np.asarray(w_out)[0]), tiles(np.asarray(peer_wq)[0])])
    k_i, w_i = w[:, c_ki:c_wi], w[:, c_wi:]
    kw = np.concatenate([k_i, k_i, w_i], 1).reshape(KC, P, KWCOL).transpose(1, 0, 2)
    x2 = np.asarray(x)[0]
    conv = np.concatenate([np.asarray(dw_w)[0], np.asarray(dw_b)], 0)
    ins = {
        "xT": x2.T.reshape(KC, P, S).transpose(1, 0, 2),
        "x_tok": x2,
        "w_stream": stream,
        "w_kw": kw,
        "w_sub": np.asarray(peer_sub_keys)[0].transpose(3, 0, 1, 2).reshape(P, 2 * PH * PK),
        "conv_p": conv.reshape(TAPS + 1, CC, P).transpose(2, 1, 0).reshape(P, -1),
        "cln": np.concatenate([cols(conv_ln_g, CC), cols(conv_ln_b, CC)], 1),
        "bucket1h": _bucket_onehot(),
        "rel_bias": np.asarray(rel_bias),
        "b_out": np.asarray(b_out),
        "ln1_col": np.stack([cols(ln1_g, KC), cols(ln1_b, KC)]),
        "ln_rows": np.concatenate([np.asarray(a) for a in (ln1_g, ln1_b, ln2_g, ln2_b)], 0),
        "u_tab": np.asarray(peer_u)[0],
        "v_tab": np.asarray(peer_v)[0],
    }
    nc = _bacc.Bacc("TRN2", target_bir_lowering=False, num_devices=1)
    arrays, args = {}, {}
    for name, a in ins.items():
        a = np.ascontiguousarray(a)
        arrays[f"in_{name}"] = a
        args[name] = nc.dram_tensor(f"in_{name}", a.shape, mybir.dt.from_np(a.dtype), kind="ExternalInput").ap()
    args["out"] = nc.dram_tensor("out_dram", (S, D), F32, kind="ExternalOutput").ap()
    layer(nc, **args)
    r = _run(nc, [arrays], core_ids=[0])
    return r.results[0]["out_dram"].reshape(1, S, D)
```

```python
from contextlib import ExitStack

import concourse.bass as bass
import numpy as np
from concourse import mybir

F32 = mybir.dt.float32
I32 = mybir.dt.int32
U32 = mybir.dt.uint32
F32R = mybir.dt.float32r
ALU = mybir.AluOpType
ACT = mybir.ActivationFunctionType
AX = mybir.AxisListType

P = 128
D = 2048
S = 256
TI = S // P
KC = D // P
DC = D // 2
CC = DC // P
TAPS = 31
HD = 64
NH = 16
NSEL = 64
BUCKETS = 32
MAX_DIST = 128
PH = 8
PK = 128
TOP = 16
SLOTS = PH * TOP
EPS = 1e-5
ALPHA = 2.0 ** 0.25
NEG = -1.0e30
FILL = -1.0e37
TAKEN = -3.0e38

UNIT = 2048
RING = 4
U_IDX, U_GLU, U_V, U_QK, U_OUT, U_WQ, U_END = 0, 8, 24, 32, 48, 64, 80
KWCOL = HD + NH
SKEW = S + P - 1

G = 4
RG = 2
GROUPS = SLOTS // G
TURNS = GROUPS // RG
AHEAD = RG
EARLY_SLOT = (0, 1, 2, 0, 1, 2, 3, 0)
EARLY_AT = (6, 7, 8, 11, 13, 14)
RANKED = ((0,), (1, 2), (3, 4), (5,), (6,), (7,))
EARLY_DOTS = (1, 3, 5, 6, 6, 6)


def layer(nc, xT, x_tok, w_stream, w_kw, w_sub, conv_p, cln, bucket1h, rel_bias,
          b_out, ln1_col, ln_rows, u_tab, v_tab, out):
    with ExitStack() as ctx:
        def sb(name, shape, dt=F32):
            return ctx.enter_context(nc.sbuf_tensor(name, shape, dt))

        def sem(name):
            return ctx.enter_context(nc.semaphore(name))

        psum = ctx.enter_context(nc.psum_tensor("psum", [P, 8, 512], F32))
        ps = [psum[:, i, :] for i in range(8)]

        def u_slot(k, j):
            return (k + 1) % RG * G + j

        def span(i):
            return slice(0, S) if i else slice(S, S + P)

        KB = 1024
        arena0 = (nc.sbuf_base + 63) // 64 * 64
        arena = sb("arena", [P, (160 * KB + 64) // 4])
        spot = {"x_hi": 0, "x_lo": 16, "w_lo": 32, "w_hi": 64, "bias": 96, "cat_hi": 112, "rows": 128, "x1": 144}

        def put(name, where, shape, dt=F32, plus=0):
            return nc.alloc_sbuf_tensor_at(name, shape, dt, offset=arena0 + (spot[where] + plus) * KB)[:]

        xh = put("xT_hi", "x_hi", [P, KC, S], F32R)
        xl = put("xT_lo", "x_lo", [P, KC, S], F32R)
        b_row = put("b_row", "x_hi", [1, D])
        w_raw = [put(f"w_raw{k}", "w_lo", [P, UNIT], plus=8 * k) for k in range(RING)]
        w_lo = [put(f"w_lo{k}", "w_lo", [P, UNIT], F32R, plus=8 * k) for k in range(RING)]
        w_hi = [put(f"w_hi{k}", "w_hi", [P, UNIT], F32R, plus=8 * k) for k in range(RING)]
        x_raw = put("xT_raw", "bias", [P, KC, S])
        bias = put("bias", "bias", [P, NH, S])
        sub = put("sub", "bias", [P, 2 * PH * PK])
        x1c = [put(f"x1T_chunks{k}", "bias", [P, 2 * S], plus=8 + 2 * k) for k in range(4)]
        skew = put("skew", "cat_hi", [P, NH, S])
        sq = put("conv_sq", "cat_hi", [P, CC, S], plus=8)
        cat_h = put("catT_hi", "cat_hi", [P, 2 * CC, S], F32R)
        kw = put("kw", "rows", [P, KC, KWCOL])
        convT = put("convT", "rows", [P, CC, S], plus=8)
        cat_l = put("catT_lo", "rows", [P, 2 * CC, S], F32R)
        rows = put("ln_rows_sb", "rows", [P, 2, D])
        v_sb = put("v_sb", "x1", [P, TI, DC])
        att = put("att", "x1", [P, TI, DC], plus=8)
        x1 = put("x1", "x1", [P, TI, D])
        places = [("cat_hi", 0, 0), ("cat_hi", 8, 0), ("bias", 8, 0)]
        places += [(w, 8 * k, U_END - RING + 1 + k) for k in range(RING) for w in ("w_lo", "w_hi")]
        places += [("x_hi", 8 * k, U_END) for k in range(4)] + [("bias", 0, U_END)]
        u_ring, v_ring = ([put(f"{n}_row{k}", w, [P, D], plus=o) for k, (w, o, _) in enumerate(part)]
                          for n, part in (("u", places[:RG * G]), ("v", places[RG * G:])))

        scratch = sb("scratch", [P, 4768])
        at = {"attention": 0, "peer": 0}

        def tmp(half, cols):
            at[half] += cols
            assert at[half] <= 4768
            return scratch[:, at[half] - cols:at[half]]

        ident = sb("ident", [P, P])
        ident_a = sb("ident_alpha", [P, P])
        flip = sb("flip", [P, P])
        mean_w = sb("mean_w", [P, P])
        ones_row = sb("ones_row", [1, P])
        iota_i = sb("iota_i", [P, TOP * TOP], I32)
        iota_f = sb("iota_f", [P, TOP * TOP])
        onehot = sb("onehot", [BUCKETS, SKEW])
        relb = sb("relb", [BUCKETS, NH])
        dist_row = sb("dist_row", [NH, SKEW])
        conv_sb = sb("conv_sb", [P, CC * (TAPS + 1)])
        conv_c = sb("conv_c", [P, TAPS + 1])
        cln_sb = sb("cln_sb", [P, 2 * CC])
        ln1c = sb("ln1c", [P, 2 * KC])
        eps = sb("eps", [P, 1])

        kidxT = sb("kidxT", [P, S])
        widxT = sb("widxT", [NH, S])
        widx = sb("widx", [P, TI * NH])
        qidx = [tmp("attention", S) for k in range(2)]
        rel = [tmp("attention", 2 * (S + P)).rearrange("p (j s) -> p j s", j=2) for k in range(2)]
        acc = [tmp("attention", P), tmp("attention", S)]
        acc_b = [tmp("attention", P), tmp("attention", S)]
        best8 = [sb("best8_0", [P, 8]), sb("best8_1", [P, 8])]
        mask = [tmp("attention", P), tmp("attention", S)]
        sig = [tmp("attention", S) for k in range(2)] + qidx
        cbuf = tmp("attention", TAPS - 1 + S)
        cacc = [tmp("attention", S) for k in range(2)]
        rstd_c = tmp("attention", S)
        at["attention"] = 0
        qT = tmp("attention", S)
        kT = tmp("attention", S)
        lg = [tmp("attention", 2 * P).rearrange("p (j s) -> p j s", j=2), tmp("attention", 2 * S).rearrange("p (j s) -> p j s", j=2)]
        mx = sb("mx", [P, 4])
        nm = sb("nm", [P, 4])
        rsum = [sb(f"rsum{k}", [P, 4]) for k in range(2)]
        rinv = sb("rinv", [P, 4])
        pT = [tmp("attention", 2 * P), tmp("attention", 4 * P)]
        assert at["attention"] <= 2 * S + 4 * (S + P)
        stats = sb("stats", [P, TI * 4, 6])
        mv = sb("mv", [P, TI, 2])
        sd = sb("sd", [P, TI])
        rstd = sb("rstd", [P, TI])
        nmr = sb("minus_mean_rstd", [P, 1])

        qc = [tmp("peer", S) for k in range(2)]
        sw = [tmp("peer", PK) for k in range(8)]
        later = sb("later", [P, 2 * PH * PK])
        sw2 = [[tmp("peer", PK) for c in range(2)] for a in range(2)]
        val, idxf, posf, pick = ([[sb(f"{n}{a}{c}", [P, TOP]) for c in range(2)] for a in range(2)]
                                 for n in ("val", "idxf", "posf", "pick"))
        idx, posp = ([[sb(f"{n}{a}{c}", [P, TOP], U32) for c in range(2)] for a in range(2)] for n in ("idx", "posp"))
        pos = [sb(f"pos{a}", [P, TOP], U32) for a in range(2)]
        cand = [[tmp("peer", TOP * TOP) for c in range(2)] for a in range(2)]
        hit = [[t.rearrange("p (r j) -> p r j", j=TOP) for t in cand[a]] for a in range(2)]
        gate = sb("gate", [P, TI, SLOTS])
        gsum = sb("gsum", [P, PH])
        ginv = sb("ginv", [P, PH])
        eid = sb("eid", [P, TI * SLOTS], I32)
        eslot = {t: [sb(f"eslot_{t}{k}", [P, G], I32) for k in range(RG)] for t in "uv"}
        dots = [sb(f"dots{k}", [P, G]) for k in range(RG)]
        gel = [sb(f"gel{k}", [P, G]) for k in range(RG)]
        weight = [sb(f"weight{k}", [P, G]) for k in range(RG)]
        diag = [tmp("peer", G * P).rearrange("p (j t) -> p j t", j=G) for k in range(RG)]

        row_scratch = nc.dram_tensor("dist_rows", (NH, SKEW), F32, kind="Internal").ap()

        x_split = sem("x_split")
        hi_done = sem("hi_done")
        lo_pool, lo_dve = sem("lo_pool"), sem("lo_dve")
        x_hi_done = sem("x_hi_done")
        att_lo, cat_lo, x1c_done, x1h_done = sem("att_lo"), sem("cat_lo"), sem("x1c_done"), sem("x1h_done")
        x_in = [sem(f"x_in{q}") for q in range(4)]
        kw_in = [sem(f"kw_in{q}") for q in range(4)]
        small_in, row_in, sub_in, b_in, row2_in = (
            sem(n) for n in ("small_in", "row_in", "sub_in", "b_in", "row2_in"))
        row1_in = sem("row1_in")
        w_in = [sem(f"w_in{k}") for k in range(RING)]
        row_out, skew_in = sem("row_out"), sem("skew_in")
        out_done = sem("out_done")
        pool_const = sem("pool_const")
        causal = sem("causal")
        dve_step = sem("dve_step")
        w_used = sem("w_used")
        kw_done, kw_copied = sem("kw_done"), sem("kw_copied")
        widxT_copied, widx_turned = sem("widxT_copied"), sem("widx_turned")
        qidx_copied, score_done, relu_done, idx_added = (sem(n) for n in ("qidx_copied", "score_done", "relu_done", "idx_added"))
        row_done, row_copied, flip_done, bias_copied = (sem(n) for n in ("row_done", "row_copied", "flip_done", "bias_copied"))
        scored, masked = sem("scored"), sem("masked")
        sig_done, glu_done, conv_done = sem("sig_done"), sem("glu_done"), sem("conv_done")
        v_copied = sem("v_copied")
        mean_done, centred, squared, var_done, sd_done, normed, conv_out = (
            sem(n) for n in ("mean_done", "centred", "squared", "var_done", "sd_done", "normed", "conv_out"))
        qk_copied, logit_done, logit_read, max_done, exp_done = (
            sem(n) for n in ("qk_copied", "logit_done", "logit_read", "max_done", "exp_done"))
        turned, pt_copied, pv_done, att_done = sem("turned"), sem("pt_copied"), sem("pv_done"), sem("att_done")
        att_turned, att_copied, mix_read = sem("att_turned"), sem("att_copied"), sem("mix_read")
        mix_done = sem("mix_done")
        var1, sd1, shift1, xn0_done, xn1_done, xn_turned, x1T_even, x1T_odd, x1_done = (
            sem(n) for n in ("var1", "sd1", "shift1", "xn0_done", "xn1_done", "xn_turned", "x1T_even", "x1T_odd", "x1_done"))
        qc_copied, key_done, key_copied, key_used = (sem(n) for n in ("qc_copied", "key_done", "key_copied", "key_used"))
        gate_sub, gate_exp, picked = sem("gate_sub"), sem("gate_exp"), sem("picked")
        eslot_done = sem("eslot_done")
        early_read = sem("early_read")
        bank_done = sem("bank_done")
        row2_done, row2_copied = sem("row2_done"), sem("row2_copied")
        u_in = [sem(f"u_in{k}") for k in range(RG * G)]
        v_in = [sem(f"v_in{k}") for k in range(RG * G)]
        dots_done, gelu_done, diag_done, y_done = (sem(n) for n in ("dots_done", "gelu_done", "diag_done", "y_done"))
        var2, sd2, res_done = sem("var2"), sem("sd2"), sem("res_done")
        passed = {e: sem(f"passed_{e}") for e in ("pe", "act", "dve", "pool")}

        block = ctx.enter_context(nc.Block())

        @block.sync
        def _(sp):
            for q in range(4):
                sp.dma_start(kw[:, 4 * q:4 * q + 4, :], w_kw[:, 4 * q:4 * q + 4, :]).then_inc(kw_in[q], 16)
                sp.dma_start(x_raw[:, 4 * q:4 * q + 4, :], xT[:, 4 * q:4 * q + 4, :]).then_inc(x_in[q], 16)
            for k in range(RING):
                sp.dma_start(w_raw[k], w_stream[k]).then_inc(w_in[k], 16)
            with sp.Fori(1, U_END // RING) as r:
                for k in range(RING):
                    sp.wait_ge(w_used, r * RING + (k - RING + 1))
                    sp.dma_start(w_raw[k], w_stream[bass.ds(r * RING + k, 1)].rearrange("a p n -> (a p) n")).then_inc(w_in[k], 16)
            sp.wait_ge(x1_done, TI)
            for k in range(2):
                sp.dma_start(rows[0:1, k, :], ln_rows[k + 2:k + 3, :]).then_inc(row2_in, 16)
            for i in range(TI):
                for n in range(4):
                    sp.wait_ge(res_done, 4 * i + n + 1)
                    sp.dma_start(out[i * P:(i + 1) * P, n * 512:(n + 1) * 512], x1[:, i, n * 512:(n + 1) * 512]).then_inc(out_done, 16)
            sp.wait_ge(out_done, 16 * 4 * TI)

        @block.gpsimd
        def _(pool):
            pool.memset(ident[:, :], 0.0)
            pool.memset(ident_a[:, :], 0.0)
            pool.memset(flip[:, :], 0.0)
            pool.memset(mean_w[:, :], 1.0 / DC)
            pool.memset(ones_row[:, :], 1.0)
            pool.memset(eps[:, :], EPS)
            pool.iota(iota_i[:, :].rearrange("p (r j) -> p r j", j=TOP), [[0, TOP], [1, TOP]], channel_multiplier=0).then_inc(pool_const, 1)
            pool.wait_ge(pool_const, 1)
            pool.affine_select(out=ident[:, :], in_=ident[:, :], compare_op=ALU.not_equal, fill=1.0,
                               base=0, pattern=[[-1, P]], channel_multiplier=1)
            pool.affine_select(out=ident_a[:, :], in_=ident_a[:, :], compare_op=ALU.not_equal, fill=ALPHA,
                               base=0, pattern=[[-1, P]], channel_multiplier=1)
            pool.affine_select(out=flip[:, :], in_=flip[:, :], compare_op=ALU.not_equal, fill=1.0,
                               base=-(P - 1), pattern=[[1, P]], channel_multiplier=1).then_inc(pool_const, 1)
            def lower(n, u, k):
                pool.wait_ge(hi_done, u + 1)
                pool.tensor_tensor(w_lo[k], w_raw[k], w_hi[k].bitcast(F32), ALU.subtract).then_inc(lo_pool, 1)

            def cut(ready, ts, fill):
                for i in range(TI):
                    pool.wait_ge(ready, i + 1)
                    pool.affine_select(out=ts[i], in_=ts[i], compare_op=ALU.is_ge, fill=fill,
                                       base=i * P, pattern=[[-1, (i + 1) * P]], channel_multiplier=1).then_inc(causal, 1)

            for m in range(2):
                lower(m, U_GLU + m, m)
            cut(scored, acc, FILL)
            for m in range(2, 4):
                lower(m, U_GLU + m, m)
            with pool.Fori(1, 4) as r:
                for k in range(RING):
                    lower(r * RING + k, r * RING + (U_GLU + k), k)
            cut(masked, mask, NEG)
            with pool.Fori(0, (U_OUT - U_V) // RING) as r:
                for k in range(RING):
                    lower(r * RING + (16 + k), r * RING + (U_V + k), k)
            pool.wait_ge(w_used, U_OUT)
            pool.dma_start(b_row, b_out).then_inc(b_in, 16)
            pool.wait_ge(logit_read, CC)
            pool.dma_start(sub, w_sub).then_inc(sub_in, 16)
            pool.wait_ge(att_turned, 4)
            pool.dma_start(x1, x_tok.rearrange("(i p) d -> p i d", p=P)).then_inc(row_in, 16)
            for k in range(2):
                lower(40 + k, U_WQ + k, k)
            pool.wait_ge(w_used, U_WQ)
            for k in range(2):
                pool.dma_start(rows[:, k, :], ln_rows[k:k + 1, :].to_broadcast([P, D])).then_inc(row1_in, 16)
            for m in range(1, KC // 2, 2):
                pool.wait_ge(x1h_done, m + 1)
                pool.tensor_tensor(xl[:, 2 * m:2 * m + 2, :].rearrange("p c t -> p (c t)"), x1c[m % 4],
                                   xh[:, 2 * m:2 * m + 2, :].rearrange("p c t -> p (c t)").bitcast(F32),
                                   ALU.subtract).then_inc(x1T_odd, 1)
            for k in range(2, RING):
                lower(40 + k, U_WQ + k, k)
            def gather(tab, dst, ids, land):
                pool.indirect_dma_start(dst, None, tab, bass.IndirectOffsetOnAxis(ap=ids, axis=0)).then_inc(land, 16)

            def early(n):
                s = EARLY_SLOT[n]
                if n == 0:
                    pool.wait_ge(picked, TURNS // PH)
                if s in EARLY_SLOT[:n]:
                    pool.wait_ge(early_read, max(m for m in range(n) if EARLY_SLOT[m] == s) + 1)
                elif places[s][2]:
                    pool.wait_ge(w_used, places[s][2])
                gather(u_tab, u_ring[s], eid[:, n:n + 1], u_in[s])

            n_early = 0
            for u in range(RING, 2 * PH):
                lower(40 + u, U_WQ + u, u % RING)
                if u in EARLY_AT:
                    early(n_early)
                    n_early += 1
            for n in range(n_early, AHEAD * G):
                early(n)

            def gather_group(g, k, tab, ring, land, t, ahead, count):
                pool.sem_inc(passed["pool"], 1)
                pool.tensor_copy(eslot[t][k][:, :], eid[:, bass.ds((g + ahead) * G, G)]).then_inc(eslot_done, 1)
                pool.wait_ge(eslot_done, count)
                pool.sem_inc(passed["pool"], 1)
                for j in range(G):
                    s = u_slot(k, j) if t == "u" else k * G + j
                    gather(tab, ring[s], eslot[t][k][:, j:j + 1], land[s])

            def u_rows(g, k, count):
                pool.wait_ge(dots_done, g + 1)
                gather_group(g, k, u_tab, u_ring, u_in, "u", AHEAD, count)

            def turn(r, with_u=True):
                for k in range(RG):
                    g = r * RG + k
                    if with_u and k == 0:
                        pool.wait_ge(picked, r + 2)
                        pool.wait_ge(w_used, U_END - 1)
                        u_rows(g, k, g * 2 + 1)
                        pool.wait_ge(w_used, U_END)
                        pool.wait_ge(key_copied, 2 + 2 * PH)
                    pool.wait_ge(y_done, g + 1)
                    gather_group(g, k, v_tab, v_ring, v_in, "v", 0,
                                 g * 2 + 2 - k if with_u else GROUPS * TI * 2 - 2 * RG + k + 1)
                    if with_u and k:
                        u_rows(g, k, g * 2 + 2)

            with pool.Fori(0, TI * TURNS - 1) as r:
                turn(r)
            turn(TI * TURNS - 1, with_u=False)

        @block.tensor
        def _(pe):
            def unit_in(lo, n):
                pe.wait_ge(lo, n + 1)

            def exact(dst, a, b, first, last):
                pe.matmul(dst, a[0], b[0], start=first, stop=False)
                pe.matmul(dst, a[0], b[1], start=False, stop=False)
                return pe.matmul(dst, a[1], b[0], start=False, stop=last)

            def project(k, dst, lo, n, x1_arrives=False):
                unit_in(lo, n)
                w = [t[k].rearrange("p (c n) -> p c n", c=KC) for t in (w_hi, w_lo)]
                for c in range(KC):
                    if x1_arrives and c % 2 == 0:
                        pe.wait_ge(x1T_odd if c % 4 else x1T_even, c // 4 + 1)
                    last = exact(dst, [t[:, c, :] for t in w], [xh[:, c, :], xl[:, c, :]], c == 0, c == KC - 1)
                last.then_inc(w_used, 1)

            for c in range(KC):
                if c % 4 == 0:
                    pe.wait_ge(kw_in[c // 4], 16)
                    pe.wait_ge(x_in[c // 4], 16)
                last = pe.matmul(ps[6][0:KWCOL, 0:S], kw[:, c, :], x_raw[:, c, :], start=c == 0, stop=c == KC - 1)
            last.then_inc(kw_done, 1)
            pe.wait_ge(small_in, 16 * 6)
            pe.matmul(ps[7][0:NH, 0:SKEW], relb[:, :], onehot[:, :], start=True, stop=True).then_inc(row_done, 1)
            pe.wait_ge(pool_const, 2)
            pe.wait_ge(widxT_copied, 1)
            for i in range(TI):
                last = pe.transpose(ps[5][:, i * NH:(i + 1) * NH], widxT[:, i * P:(i + 1) * P], ident[0:NH, 0:NH])
            last.then_inc(widx_turned, 1)
            pe.wait_ge(kw_copied, 3)
            pe.wait_ge(x_split, 4)

            def index_scores(u, k):
                pe.wait_ge(qidx_copied, u + 3)
                pe.wait_ge(relu_done, u + 1)
                for i in range(TI):
                    for j in range(2):
                        n = (i + 1) * P
                        last = pe.matmul(ps[2 + 2 * j + k % 2][:, span(i)],
                                         qidx[k % 2][j * HD:(j + 1) * HD, i * P:(i + 1) * P],
                                         kidxT[j * HD:(j + 1) * HD, 0:n], start=True, stop=True)
                last.then_inc(score_done, 1)

            with pe.Fori(0, CC // RING) as r:
                for k in range(RING):
                    u = r * RING + k
                    pe.wait_ge(qidx_copied, u + 1)
                    project(k, ps[k % 2][:, 0:S], lo_dve, u)
                    if k:
                        index_scores(u - 1, k - 1)
                index_scores(r * RING + (RING - 1), RING - 1)

            pe.wait_ge(skew_in, 16)
            pe.wait_ge(pool_const, 2)
            for n in range(8):
                pe.wait_ge(bias_copied, max(n - 1, 0))
                pe.matmul(ps[6 + n % 2][:, :], flip[:, :], skew[:, 2 * n:2 * n + 2, :].rearrange("p h s -> p (h s)"),
                          start=True, stop=True).then_inc(flip_done, 1)

            pe.wait_ge(relu_done, CC + 2)
            with pe.Fori(0, CC // 4) as r:
                for k in range(4):
                    pe.wait_ge(glu_done, r * 4 + (k + 1))
                    if k == 3:
                        pe.wait_ge(bias_copied, 8)
                    for half in range(2):
                        s = 2 * k + half
                        project(s % RING, ps[s][:, 0:S], lo_pool, r * 8 + s)

            for n in range(2):
                pe.wait_ge(glu_done, 4 + CC // 2 + 1 + n)
                for q in range(RING):
                    unit_in(lo_pool, 16 + n * RING + q)
                    w = [t[q].rearrange("p (c n) -> p c n", c=4) for t in (w_hi, w_lo)]
                    for c in range(4):
                        for i in range(TI):
                            last = exact(ps[2 * n + i], [t[:, 4 * q + c, i * P:(i + 1) * P] for t in (xh, xl)],
                                         [t[:, c, :] for t in w], q + c == 0, q + c == 6)
                    last.then_inc(w_used, 1)

            def qk(hp, k):
                pe.wait_ge(qk_copied, hp * 2)
                project(2 * k, ps[0][:, 0:S], lo_pool, hp * 2 + 24)
                project(2 * k + 1, ps[1][:, 0:S], lo_pool, hp * 2 + 25)

            def logits(hp):
                pe.wait_ge(qk_copied, hp * 2 + 2)
                pe.wait_ge(logit_read, hp)
                for i in range(TI):
                    n = (i + 1) * P
                    for j in range(2):
                        last = pe.matmul(ps[2 + j][:, span(i)], qT[j * HD:(j + 1) * HD, i * P:(i + 1) * P],
                                         kT[j * HD:(j + 1) * HD, 0:n], start=True, stop=True)
                last.then_inc(logit_done, 1)

            def turn(hp):
                pe.wait_ge(exp_done, hp * 4 + 4)
                for i in range(TI):
                    for j in range(2):
                        for b in range(i + 1):
                            last = pe.transpose(ps[4 + i][:, (j * (i + 1) + b) * P:(j * (i + 1) + b + 1) * P],
                                                lg[i][:, j, b * P:(b + 1) * P], ident[:, :])
                last.then_inc(turned, 1)

            def values(hp):
                pe.wait_ge(pt_copied, hp * 2 + 2)
                pe.wait_ge(att_done, hp + 1)
                for i in range(TI):
                    for j in range(2):
                        for b in range(i + 1):
                            last = pe.matmul(ps[6][:, (2 * i + j) * HD:(2 * i + j + 1) * HD],
                                             pT[i][:, (j * (i + 1) + b) * P:(j * (i + 1) + b + 1) * P],
                                             v_sb[:, b, bass.ds(hp * P + j * HD, HD)], start=b == 0, stop=b == i)
                last.then_inc(pv_done, 1)

            pe.wait_ge(v_copied, 2)
            project(0, ps[0][:, 0:S], lo_pool, 24)
            pe.wait_ge(conv_done, CC)
            for c in range(CC):
                last = pe.matmul(ps[7][:, 0:S], mean_w[:, :], convT[:, c, :], start=c == 0, stop=c == CC - 1)
            last.then_inc(mean_done, 1)
            project(1, ps[1][:, 0:S], lo_pool, 25)
            pe.wait_ge(squared, 1)
            for c in range(CC):
                last = pe.matmul(ps[7][:, 0:S], mean_w[:, :], sq[:, c, :], start=c == 0, stop=c == CC - 1)
            last.then_inc(var_done, 1)
            pe.wait_ge(v_copied, 4)
            logits(0)
            with pe.Fori(0, 3) as r:
                for k in range(2):
                    hp = r * 2 + (k + 1)
                    qk(hp, 1 - k)
                    turn(hp - 1)
                    logits(hp)
                    values(hp - 1)
            qk(7, 1)
            turn(6)
            logits(7)
            values(6)

            def mix(n, q, chunks, tiles=range(TI)):
                bank = 6 if n % 2 else 0
                unit_in(lo_dve, 8 + n * RING + q)
                w = [t[q].rearrange("p (c n) -> p c n", c=4) for t in (w_hi, w_lo)]
                for c in chunks:
                    for i in tiles:
                        last = exact(ps[bank + i], [t[:, 4 * q + c, i * P:(i + 1) * P] for t in (cat_h, cat_l)],
                                     [t[:, c, :] for t in w], q + c == 0, False)
                if chunks[-1] == 3 and tiles[-1] == TI - 1:
                    last.then_inc(w_used, 1)

            pe.wait_ge(qk_copied, 2 * CC)
            pe.wait_ge(cat_lo, CC)
            mix(0, 0, range(4))
            turn(7)
            mix(0, 1, range(2))
            values(7)
            mix(0, 1, range(2, 4))

            pe.wait_ge(att_done, CC + 1)
            for m in range(4):
                for c in range(2):
                    for i in range(TI):
                        last = pe.transpose(ps[2 + m][:, (2 * c + i) * P:(2 * c + i + 1) * P],
                                            att[:, i, (2 * m + c) * P:(2 * m + c + 1) * P], ident[:, :])
                last.then_inc(att_turned, 1)

            for n in range(4):
                bank = 6 if n % 2 else 0
                pe.wait_ge(mix_read, max(n - 1, 0) * TI)
                for q in range(RING) if n else (2, 3):
                    if n == 0:
                        pe.wait_ge(att_lo, 2 * (q - 1))
                    if (n, q) != (3, RING - 1):
                        mix(n, q, range(4))
                pe.wait_ge(b_in, 16)
                for i in range(TI):
                    if n == 3:
                        mix(n, RING - 1, range(4), (i,))
                    pe.matmul(ps[bank + i], ones_row[:, :], b_row[:, n * 512:(n + 1) * 512], start=False, stop=True).then_inc(mix_done, 1)

            for m in range(KC // 2):
                pe.wait_ge(xn0_done, m // 2 + 1)
                pe.wait_ge(xn1_done, m // 2 + 1)
                pe.wait_ge(x1c_done, max(m - 3, 0))
                for c in range(2):
                    for i in range(TI):
                        last = pe.transpose(ps[2 + m % 4][:, (2 * c + i) * P:(2 * c + i + 1) * P],
                                            x1[:, i, (2 * m + c) * P:(2 * m + c + 1) * P], ident[:, :])
                last.then_inc(xn_turned, 1)

            def key_scores(u, k):
                pe.wait_ge(qc_copied, u + 3)
                pe.wait_ge(key_copied, u + 1)
                for i in range(TI):
                    last = pe.matmul(ps[2 + k % 2][:, i * PK:(i + 1) * PK], qc[k % 2][:, i * P:(i + 1) * P],
                                     sub[:, bass.ds(u * PK, PK)], start=True, stop=True)
                last.then_inc(key_done, 1)

            pe.wait_ge(mix_read, 8)
            pe.wait_ge(sub_in, 16)
            with pe.Fori(0, 2 * PH // RING) as r:
                for k in range(RING):
                    u = r * RING + k
                    pe.wait_ge(qc_copied, u + 1)
                    project(k, ps[k % 2][:, 0:S], lo_pool, u + 40, k == 0)
                    if k:
                        key_scores(u - 1, k - 1)
                key_scores(r * RING + (RING - 1), RING - 1)

            def add_rows(i, r, k, banks):
                g = r * RG + (k + i * GROUPS)
                pe.wait_ge(diag_done, g + 1)
                for j in range(G):
                    pe.wait_ge(v_in[k * G + j], r * 16 + (16 + 16 * i * TURNS))
                    for n in range(banks):
                        last = pe.matmul(ps[4 * i + n][:, :], diag[k][:, j, :], v_ring[k * G + j][:, n * 512:(n + 1) * 512],
                                         start=False, stop=True, skip_group_check=True)
                        if banks < 4 and (k, j) == (RG - 1, G - 1):
                            last.then_inc(bank_done, 1)
                if banks == 4:
                    last.then_inc(y_done, 1)

            pe.wait_ge(row2_in, 32)
            for k in range(2):
                pe.wait_ge(row2_copied, 4 * k)
                for n in range(4):
                    pe.matmul(ps[4 + n][:, :], ones_row[:, :], rows[0:1, k, n * 512:(n + 1) * 512],
                              start=True, stop=True).then_inc(row2_done, 1)

            for i in range(TI):
                pe.wait_ge(x1_done, i + 1)
                if i == 0:
                    pe.wait_ge(key_copied, 2 * PH + 2)
                for n in range(4):
                    pe.matmul(ps[4 * i + n][:, :], ident_a[:, :], x1[:, i, n * 512:(n + 1) * 512], start=True, stop=False,
                              skip_group_check=True)
                with pe.Fori(0, TURNS - i) as r:
                    for k in range(RG):
                        add_rows(i, r, k, 4)
            for k in range(RG):
                add_rows(1, TURNS - 1, k, 3)

        @block.scalar
        def _(act):
            act.dma_start(relb[:, :], rel_bias).then_inc(small_in, 16)
            act.dma_start(onehot[:, :], bucket1h).then_inc(small_in, 16)
            act.dma_start(conv_sb[:, :], conv_p).then_inc(small_in, 16)
            act.dma_start(cln_sb[:, :], cln).then_inc(small_in, 16)
            act.dma_start(ln1c[:, 0:KC], ln1_col[0]).then_inc(small_in, 16)
            act.dma_start(ln1c[:, KC:2 * KC], ln1_col[1]).then_inc(small_in, 16)
            act.sem_inc(qidx_copied, 2)
            act.sem_inc(relu_done, 2)
            act.sem_inc(qc_copied, 2)
            act.sem_inc(key_copied, 2)

            def upper(u, k):
                act.wait_ge(w_in[k], (u - k) * (16 // RING) + 16)
                if not isinstance(u, int) or u >= RING:
                    act.wait_ge(w_used, u - (RING - 1))
                    if not isinstance(u, int):
                        act.sem_inc(passed["act"], 1)
                act.activation(w_hi[k], w_raw[k], ACT.Copy).then_inc(hi_done, 1)

            for q in range(4):
                act.wait_ge(x_in[q], 16)
                act.activation(xh[:, 4 * q:4 * q + 4, :], x_raw[:, 4 * q:4 * q + 4, :], ACT.Copy).then_inc(x_hi_done, 1)
            upper(0, 0)
            act.wait_ge(kw_done, 1)
            act.activation(widxT[:, :], ps[6][HD:KWCOL, 0:S], ACT.Copy).then_inc(widxT_copied, 1)
            for half in range(2):
                act.activation(kidxT[half * HD:(half + 1) * HD, :], ps[6][0:HD, 0:S], ACT.Copy).then_inc(kw_copied, 1)
            act.wait_ge(widx_turned, 1)
            act.activation(widx[:, :], ps[5][:, 0:TI * NH], ACT.Copy).then_inc(kw_copied, 1)
            upper(1, 1)

            def relu(u):
                b = u % 2
                act.wait_ge(score_done, u + 1)
                if u >= 2:
                    act.wait_ge(idx_added, u - 1)
                for j in range(2):
                    last = act.activation(rel[b][:, j, :], ps[2 + 2 * j + b][:, 0:S + P], ACT.Relu)
                last.then_inc(relu_done, 1)

            act.wait_ge(row_done, 1)
            act.activation(dist_row[:, :], ps[7][0:NH, 0:SKEW], ACT.Copy).then_inc(row_copied, 1)
            act.wait_ge(row_copied, 1)
            act.dma_start(row_scratch, dist_row[:, :]).then_inc(row_out, 16)

            for u in range(CC):
                upper(u + 2, (u + 2) % RING)
                if u == 2:
                    act.wait_ge(row_out, 16)
                    act.dma_start(skew, bass.AP(tensor=row_scratch.tensor, offset=0, ap=[[1, P], [SKEW, NH], [1, S]])).then_inc(skew_in, 16)
                act.wait_ge(w_used, U_IDX + u + 1)
                if u >= 2:
                    act.wait_ge(score_done, u - 1)
                act.activation(qidx[u % 2][:, :], ps[u % 2][:, 0:S], ACT.Copy).then_inc(qidx_copied, 1)
                if u % RING:
                    relu(u - 1)
                if u % RING == RING - 1:
                    relu(u)

            for n in range(8):
                act.wait_ge(flip_done, n + 1)
                act.activation(bias[:, 2 * n:2 * n + 2, :].rearrange("p h s -> p (h s)"), ps[6 + n % 2][:, :], ACT.Copy).then_inc(bias_copied, 1)

            for c in range(CC):
                upper(U_GLU + 2 * c + 2, (2 * c + 2) % RING)
                upper(U_GLU + 2 * c + 3, (2 * c + 3) % RING)
                act.wait_ge(w_used, U_GLU + 2 * c + 2)
                if c >= 4:
                    act.wait_ge(glu_done, 4 + c - 3)
                act.activation(sig[c % 4][:, :], ps[2 * (c % 4) + 1][:, 0:S], ACT.Sigmoid).then_inc(sig_done, 1)

            for n in range(2):
                for q in range(RING):
                    upper(U_V + RING * n + 2 + q, (2 + q) % RING)
                act.wait_ge(w_used, U_V + RING * (n + 1))
                for i in range(TI):
                    act.activation(v_sb[:, i, n * 512:(n + 1) * 512], ps[2 * n + i][:, :], ACT.Copy).then_inc(v_copied, 1)

            act.wait_ge(centred, 1)
            act.activation(sq.rearrange("p c t -> p (c t)"), convT.rearrange("p c t -> p (c t)"), ACT.Square).then_inc(squared, 1)

            def qk_copy(hp, k):
                upper(hp * 2 + (U_QK + 2), (2 * k + 2) % RING)
                upper(hp * 2 + (U_QK + 3), (2 * k + 3) % RING)
                act.wait_ge(w_used, hp * 2 + (U_QK + 1))
                act.wait_ge(logit_done, hp)
                act.activation(qT[:, :], ps[0][:, 0:S], ACT.Copy, scale=HD ** -0.5).then_inc(qk_copied, 1)
                act.wait_ge(w_used, hp * 2 + (U_QK + 2))
                act.activation(kT[:, :], ps[1][:, 0:S], ACT.Copy).then_inc(qk_copied, 1)

            def exps(hp, b):
                act.wait_ge(max_done, hp + 1)
                for i in range(TI):
                    for j in range(2):
                        a = 2 * i + j
                        act.activation(lg[i][:, j, :], lg[i][:, j, :], ACT.Exp, bias=nm[:, a:a + 1],
                                       accum_out=rsum[b][:, a:a + 1]).then_inc(exp_done, 1)

            def pt_copy(hp):
                act.wait_ge(turned, hp + 1)
                act.wait_ge(pv_done, hp + 1)
                act.activation(pT[0][:, :], ps[4][:, 0:2 * P], ACT.Copy).then_inc(pt_copied, 1)
                act.activation(pT[1][:, :], ps[5][:, :], ACT.Copy).then_inc(pt_copied, 1)

            qk_copy(0, 0)
            act.wait_ge(var_done, 1)
            act.activation(rstd_c[:, :], ps[7][:, 0:S], ACT.Sqrt, bias=eps[:, :]).then_inc(sd_done, 1)
            act.wait_ge(normed, 1)
            for c in range(CC):
                act.activation(convT[:, c, :], convT[:, c, :], ACT.Silu, scale=cln_sb[:, c:c + 1],
                               bias=cln_sb[:, CC + c:CC + c + 1]).then_inc(conv_out, 1)
            exps(0, 0)
            with act.Fori(0, 3) as r:
                for k in range(2):
                    hp = r * 2 + (k + 1)
                    qk_copy(hp, 1 - k)
                    pt_copy(hp - 1)
                    exps(hp, 1 - k)
            qk_copy(7, 1)
            pt_copy(6)
            exps(7, 1)
            upper(U_OUT + 2, 2)
            pt_copy(7)
            upper(U_OUT + 3, 3)

            for m in range(4):
                act.wait_ge(att_turned, m + 1)
                act.activation(cat_h[:, CC + 2 * m:CC + 2 * m + 2, :].rearrange("p c t -> p (c t)"), ps[2 + m], ACT.Copy).then_inc(att_copied, 1)
            for u in range(U_OUT + RING, U_WQ + 2):
                upper(u, u % RING)

            def sd_1(i):
                act.wait_ge(var1, i + 1)
                act.activation(sd[:, i:i + 1], mv[:, i, 1:2], ACT.Sqrt, bias=eps[:, :]).then_inc(sd1, 1)

            sd_1(0)
            act.wait_ge(shift1, 1)
            for n in range(4):
                if n == 3:
                    sd_1(1)
                x_n = x1[:, 0, n * 512:(n + 1) * 512]
                act.activation(x_n, x_n, ACT.Identity, scale=rstd[:, 0:1], bias=nmr[:, :]).then_inc(xn0_done, 1)
            for m in range(KC // 2):
                act.wait_ge(x1c_done, m + 1)
                act.activation(xh[:, 2 * m:2 * m + 2, :].rearrange("p c t -> p (c t)"), x1c[m % 4], ACT.Copy).then_inc(x1h_done, 1)

            def key_copy(u):
                act.wait_ge(key_done, u + 1)
                if u >= 8:
                    act.wait_ge(key_used, u // 2 - 3)
                act.activation(sw[u % 8], ps[2 + u % 2][:, 0:PK], ACT.Copy)
                act.activation(later[:, u * PK:(u + 1) * PK], ps[2 + u % 2][:, PK:2 * PK], ACT.Copy).then_inc(key_copied, 1)

            def gate_exps(n, i, first, end):
                act.wait_ge(gate_sub, n + 1)
                g = gate[:, i, first * TOP:end * TOP]
                act.activation(g, g, ACT.Exp).then_inc(gate_exp, 1)

            for u in range(2 * PH):
                if u == 2 * PH - 2:
                    gate_exps(0, 0, 0, PH // 2)
                if U_WQ + u + 2 < U_END:
                    upper(U_WQ + u + 2, (u + 2) % RING)
                act.wait_ge(w_used, U_WQ + u + 1)
                if u >= 2:
                    act.wait_ge(key_done, u - 1)
                act.activation(qc[u % 2][:, :], ps[u % 2][:, 0:S], ACT.Copy).then_inc(qc_copied, 1)
                if u % RING:
                    key_copy(u - 1)
                if u % RING == RING - 1:
                    key_copy(u)

            def gelu(n, k):
                act.wait_ge(dots_done, n + 1)
                act.activation(gel[k][:, :], dots[k][:, :], ACT.Gelu).then_inc(gelu_done, 1)

            def gelus(first, last):
                with act.Fori(first, last) as r:
                    for k in range(RG):
                        gelu(r * RG + (k + AHEAD), k)

            def sd_rows(i):
                act.wait_ge(var2, i + 1)
                act.activation(sd[:, i:i + 1], mv[:, i, 1:2], ACT.Sqrt, bias=eps[:, :]).then_inc(sd2, 1)

            for n in range(8):
                act.wait_ge(row2_done, n + 1)
                act.activation(rows[:, n // 4, n % 4 * 512:(n % 4 + 1) * 512], ps[4 + n % 4][:, :], ACT.Copy).then_inc(row2_copied, 1)

            for k in range(AHEAD):
                gelu(k, k)
            gelus(0, TURNS // PH)
            gate_exps(1, 0, PH // 2, PH)
            gelus(TURNS // PH, TURNS)
            gate_exps(2, 1, 0, PH)
            gelus(TURNS, TURNS + 2)
            sd_rows(0)
            gelus(TURNS + 2, TI * TURNS - 1)
            sd_rows(1)

        @block.vector
        def _(dve):
            steps = [0]

            def link(ins):
                steps[0] += 1
                ins.then_inc(dve_step, 1)
                dve.wait_ge(dve_step, steps[0])

            dve.sem_inc(glu_done, 4)
            dve.sem_inc(y_done, RG)
            dve.sem_inc(att_done, 1)
            dve.sem_inc(pv_done, 1)
            dve.memset(cbuf[:, :], 0.0)
            for i in range(TI):
                dve.memset(acc[i][:, :], 0.0)
            dve.wait_ge(pool_const, 1)
            link(dve.tensor_copy(iota_f[:, :], iota_i[:, :]))

            def lower(u):
                k = u % RING
                dve.wait_ge(hi_done, u + 1)
                dve.tensor_tensor(w_lo[k], w_raw[k], w_hi[k].bitcast(F32), ALU.subtract).then_inc(lo_dve, 1)

            for q in range(4):
                dve.wait_ge(x_hi_done, q + 1)
                dve.tensor_tensor(xl[:, 4 * q:4 * q + 4, :], x_raw[:, 4 * q:4 * q + 4, :], xh[:, 4 * q:4 * q + 4, :].bitcast(F32),
                                  ALU.subtract).then_inc(x_split, 1)
            lower(0)
            lower(1)

            dve.wait_ge(kw_copied, 3)
            for u in range(CC):
                if u + 2 < CC:
                    lower(u + 2)
                dve.wait_ge(relu_done, 2 + u + 1)
                for j in range(2):
                    for i in range(TI):
                        h = i * NH + 2 * u + j
                        last = dve.scalar_tensor_tensor(out=acc[i][:, :], in0=rel[u % 2][:, j, span(i)], scalar=widx[:, h:h + 1],
                                                        in1=acc[i][:, :], op0=ALU.mult, op1=ALU.add)
                    if j == 0:
                        link(last)
                last.then_inc(idx_added, 1)
                dve.wait_ge(idx_added, u + 1)
            for i in range(TI):
                dve.sem_inc(scored, 1)
            dve.wait_ge(causal, TI)
            a, b = acc, acc_b
            for n in range(NSEL // 8):
                for i in range(TI):
                    last = dve.max(best8[i][:, :], a[i][:, :])
                link(last)
                for i in range(TI):
                    last = dve.match_replace(b[i][:, :], best8[i][:, :], a[i][:, :], TAKEN)
                link(last)
                a, b = b, a
            for i in range(TI):
                dve.tensor_scalar(mask[i][:, :], a[i][:, :], TAKEN / 2, NEG, ALU.is_gt, ALU.mult).then_inc(masked, 1)

            dve.wait_ge(small_in, 16 * 6)
            for c in range(CC):
                dve.wait_ge(sig_done, c + 1)
                dve.tensor_copy(conv_c[:, :], conv_sb[:, c * (TAPS + 1):(c + 1) * (TAPS + 1)])
                dve.tensor_tensor(cbuf[:, TAPS - 1:], ps[2 * (c % 4)][:, 0:S], sig[c % 4][:, :], ALU.mult).then_inc(glu_done, 1)
                dve.wait_ge(glu_done, 4 + c + 1)
                dve.tensor_scalar(cacc[0], cbuf[:, 0:S], conv_c[:, 0:1], conv_c[:, TAPS:TAPS + 1], ALU.mult, ALU.add)
                link(dve.tensor_scalar(cacc[1], cbuf[:, 1:S + 1], conv_c[:, 1:2], None, ALU.mult))
                for t in range(2, TAPS):
                    last = dve.scalar_tensor_tensor(out=cacc[t % 2], in0=cbuf[:, t:t + S], scalar=conv_c[:, t:t + 1],
                                                    in1=cacc[t % 2], op0=ALU.mult, op1=ALU.add)
                    if t % 2 or t == TAPS - 1:
                        link(last)
                dve.tensor_tensor(convT[:, c, :], cacc[0], cacc[1], ALU.add).then_inc(conv_done, 1)
                dve.wait_ge(conv_done, c + 1)

            dve.wait_ge(mean_done, 1)
            for c in range(CC):
                last = dve.tensor_tensor(convT[:, c, :], convT[:, c, :], ps[7][:, 0:S], ALU.subtract)
            last.then_inc(centred, 1)

            def softmax_in(hp):
                dve.wait_ge(logit_done, hp + 1)
                for i in range(TI):
                    last = dve.tensor_tensor(lg[i][:, :, :], psum[:, 2:4, span(i)],
                                             bias[:, 2 * hp:2 * hp + 2, P - i * P:S], ALU.add)
                last.then_inc(logit_read, 1)
                dve.wait_ge(logit_read, hp + 1)
                for i in range(TI):
                    for j in range(2):
                        last = dve.tensor_tensor_reduce(lg[i][:, j, :], lg[i][:, j, :], mask[i][:, :], 1.0, -3.4e38,
                                                        ALU.add, ALU.max, mx[:, 2 * i + j:2 * i + j + 1])
                link(last)
                dve.tensor_scalar(nm[:, :], mx[:, :], -1.0, None, ALU.mult).then_inc(max_done, 1)

            def heads_out(hp):
                dve.wait_ge(pv_done, hp + 2)
                link(dve.reciprocal(rinv[:, :], rsum[hp % 2][:, :]))
                dve.tensor_tensor(att[:, :, hp * P:(hp + 1) * P].rearrange("p i (j d) -> p i j d", j=2),
                                  ps[6][:, 0:4 * HD].rearrange("p (i j d) -> p i j d", i=2, j=2),
                                  rinv[:, :].rearrange("p (i j o) -> p i j o", i=2, o=1).to_broadcast([P, 2, 2, HD]),
                                  ALU.mult).then_inc(att_done, 1)

            dve.wait_ge(sd_done, 1)
            link(dve.reciprocal(cacc[0], rstd_c[:, :]))
            dve.wait_ge(squared, 1)
            for c in range(CC):
                last = dve.tensor_tensor(convT[:, c, :], convT[:, c, :], cacc[0], ALU.mult)
            last.then_inc(normed, 1)
            dve.wait_ge(bias_copied, 8)
            dve.wait_ge(causal, 2 * TI)
            softmax_in(0)
            dve.wait_ge(conv_out, CC)
            link(dve.tensor_copy(cat_h[:, 0:CC, :], convT))
            dve.tensor_tensor(cat_l[:, 0:CC, :], convT, cat_h[:, 0:CC, :].bitcast(F32), ALU.subtract).then_inc(cat_lo, CC)
            for hp in range(1, CC):
                if hp == CC - 1:
                    lower(U_OUT)
                softmax_in(hp)
                if hp == CC - 1:
                    lower(U_OUT + 1)
                heads_out(hp - 1)
            heads_out(CC - 1)
            lower(U_OUT + 2)
            for m in range(4):
                dve.wait_ge(att_copied, m + 1)
                if m == 0:
                    dve.wait_ge(cat_lo, CC)
                c0 = CC + 2 * m
                dve.tensor_tensor(cat_l[:, c0:c0 + 2, :].rearrange("p c t -> p (c t)"), ps[2 + m],
                                  cat_h[:, c0:c0 + 2, :].rearrange("p c t -> p (c t)").bitcast(F32), ALU.subtract).then_inc(att_lo, 1)

            def last_stats(i):
                dve.wait_ge(mix_read, 3 * TI + i + 1)
                link(dve.bn_stats(stats[:, 4 * i + 3, :], x1[:, i, 3 * 512:D]))
                dve.bn_aggr(mv[:, i, :], stats[:, 4 * i:4 * i + 4, :]).then_inc(var1, 1)
                dve.wait_ge(sd1, i + 1)
                link(dve.reciprocal(rstd[:, i:i + 1], sd[:, i:i + 1]))
                if i == 0:
                    dve.scalar_tensor_tensor(out=nmr[:, :], in0=mv[:, 0, 0:1], scalar=-1.0, in1=rstd[:, 0:1],
                                             op0=ALU.mult, op1=ALU.mult).then_inc(shift1, 1)

            for n in range(4):
                for q in range(RING):
                    if 2 < RING * n + q + 2 < U_WQ - U_OUT:
                        lower(U_OUT + RING * n + q + 2)
                if n == 0:
                    dve.wait_ge(row_in, 16)
                for i in range(TI):
                    x_n = x1[:, i, n * 512:(n + 1) * 512]
                    dve.wait_ge(mix_done, TI * n + i + 1)
                    dve.scalar_tensor_tensor(out=x_n, in0=x_n, scalar=ALPHA, in1=ps[(6 if n % 2 else 0) + i][:, :],
                                             op0=ALU.mult, op1=ALU.add).then_inc(mix_read, 1)
                    if n == 3:
                        last_stats(i)
                if n < 3:
                    dve.wait_ge(mix_read, TI * (n + 1))
                    for i in range(TI):
                        last = dve.bn_stats(stats[:, 4 * i + n, :], x1[:, i, n * 512:(n + 1) * 512])
            for n in range(4):
                x_n = x1[:, 1, n * 512:(n + 1) * 512]
                dve.tensor_scalar(x_n, x_n, mv[:, 1, 0:1], rstd[:, 1:2], ALU.subtract, ALU.mult).then_inc(xn1_done, 1)

            def x1_lower(m):
                dve.wait_ge(x1h_done, m + 1)
                dve.tensor_tensor(xl[:, 2 * m:2 * m + 2, :].rearrange("p c t -> p (c t)"), x1c[m % 4],
                                  xh[:, 2 * m:2 * m + 2, :].rearrange("p c t -> p (c t)").bitcast(F32),
                                  ALU.subtract).then_inc(x1T_even, 1)

            for m in range(KC // 2):
                dve.wait_ge(xn_turned, m + 1)
                if m % 2 and m > 4:
                    dve.wait_ge(x1T_odd, (m - 3) // 2)
                for c in range(2):
                    kc = 2 * m + c
                    last = dve.tensor_scalar(x1c[m % 4][:, c * S:(c + 1) * S], ps[2 + m % 4][:, c * S:(c + 1) * S],
                                             ln1c[:, kc:kc + 1], ln1c[:, KC + kc:KC + kc + 1], ALU.mult, ALU.add)
                last.then_inc(x1c_done, 1)
                if m % 2:
                    x1_lower(m - 1)
            dve.wait_ge(xn0_done, 4)
            dve.wait_ge(xn1_done, 4)
            def x1_gain(i):
                link(dve.tensor_tensor(x1[:, i, :], x1[:, i, :], rows[:, 0, :], ALU.mult))
                dve.tensor_tensor(x1[:, i, :], x1[:, i, :], rows[:, 1, :], ALU.add).then_inc(x1_done, 1)
                dve.wait_ge(x1_done, i + 1)

            dve.wait_ge(row1_in, 32)
            x1_gain(0)

            def top16(jobs):
                for v, _, src, _ in jobs:
                    last = dve.max(v[:, 0:8], src)
                link(last)
                for v, ids, src, buf in jobs:
                    dve.max_index(ids[:, 0:8], v[:, 0:8], src)
                    last = dve.match_replace(buf, v[:, 0:8], src, TAKEN)
                link(last)
                for v, _, _, buf in jobs:
                    last = dve.max(v[:, 8:16], buf)
                link(last)
                for v, ids, _, buf in jobs:
                    last = dve.max_index(ids[:, 8:16], v[:, 8:16], buf)
                return last

            square = [P, TOP, TOP]
            iota_v = iota_f[:, :].rearrange("p (r j) -> p r j", j=TOP)

            def across(t):
                return t.rearrange("p (r o) -> p r o", o=1).to_broadcast(square)

            def down(t):
                return t.rearrange("p (o j) -> p o j", o=1).to_broadcast(square)

            def retrieve(i, heads, half):
                every = [(a, h, c) for a, h in enumerate(heads) for c in range(2)]
                last = top16([(val[a][c][:, :], idx[a][c][:, :], half(h, c), sw2[a][c]) for a, h, c in every])
                last.then_inc(key_used, len(heads))
                dve.wait_ge(key_used, i * PH + heads[-1] + 1)
                for a, h in enumerate(heads):
                    last = dve.tensor_tensor(cand[a][0].rearrange("p (a b) -> p a b", a=TOP), across(val[a][0][:, :]),
                                             down(val[a][1][:, :]), ALU.add)
                link(last)
                link(top16([(gate[:, i, h * TOP:(h + 1) * TOP], pos[a][:, :], cand[a][0], cand[a][1]) for a, h in enumerate(heads)]))
                for a, h in enumerate(heads):
                    dve.tensor_scalar(posp[a][0][:, :], pos[a][:, :], 4, None, ALU.logical_shift_right)
                    dve.tensor_scalar(posp[a][1][:, :], pos[a][:, :], TOP - 1, None, ALU.bitwise_and)
                for a, h, c in every:
                    last = dve.tensor_copy(idxf[a][c][:, :], idx[a][c][:, :])
                link(last)
                for a, h, c in every:
                    last = dve.tensor_copy(posf[a][c][:, :], posp[a][c][:, :])
                link(last)
                for a, h, c in every:
                    last = dve.tensor_tensor(hit[a][c], across(posf[a][c][:, :]), iota_v, ALU.is_equal)
                link(last)
                for a, h, c in every:
                    last = dve.tensor_tensor(hit[a][c], hit[a][c], down(idxf[a][c][:, :]), ALU.mult)
                link(last)
                for a, h, c in every:
                    last = dve.tensor_reduce(pick[a][c][:, :], hit[a][c], AX.X, ALU.add)
                link(last)
                for a, h in enumerate(heads):
                    last = dve.scalar_tensor_tensor(out=eid[:, i * SLOTS + h * TOP:i * SLOTS + (h + 1) * TOP], in0=pick[a][0][:, :],
                                                    scalar=float(PK), in1=pick[a][1][:, :], op0=ALU.mult, op1=ALU.add)
                link(last)
                dve.sem_inc(picked, len(heads) * TURNS // PH)

            n_gates = [0]

            def gates(i, first, end):
                n_gates[0] += 1
                g = gate[:, i, first * TOP:end * TOP].rearrange("p (h r) -> p h r", r=TOP)
                part = slice(0, end - first)
                wide = [P, end - first, TOP]
                link(dve.tensor_copy(gsum[:, part], g[:, :, 0]))
                dve.tensor_tensor(g, g, gsum[:, part].rearrange("p (a o) -> p a o", o=1).to_broadcast(wide), ALU.subtract).then_inc(gate_sub, 1)
                dve.wait_ge(gate_exp, n_gates[0])
                link(dve.tensor_reduce(gsum[:, part], g, AX.X, ALU.add))
                link(dve.reciprocal(ginv[:, part], gsum[:, part]))
                link(dve.tensor_tensor(g, g, ginv[:, part].rearrange("p (a o) -> p a o", o=1).to_broadcast(wide), ALU.mult))

            def dot(s, land, i, dst):
                dve.wait_ge(u_in[s], land)
                return dve.tensor_tensor_reduce(u_ring[s], u_ring[s], x1[:, i, :], 1.0, 0.0, ALU.mult, ALU.add, dst)

            def early_dot(n):
                s = EARLY_SLOT[n]
                ins = dot(s, 16 * EARLY_SLOT[:n + 1].count(s), 0, dots[n // G][:, n % G:n % G + 1])
                ins.then_inc(early_read, 1)
                if n % G == G - 1:
                    dve.wait_ge(early_read, n + 1)
                    dve.sem_inc(dots_done, 1)

            n_dots = 0
            for heads, done in zip(RANKED, EARLY_DOTS):
                dve.wait_ge(key_copied, 2 + 2 * heads[-1] + 2)
                retrieve(0, heads, lambda h, c: sw[(2 * h + c) % 8])
                if heads[0] == 0:
                    x1_gain(1)
                if heads[-1] == PH // 2:
                    gates(0, 0, PH // 2)
                for n in range(n_dots, done):
                    early_dot(n)
                n_dots = done
            for n in range(n_dots, AHEAD * G):
                early_dot(n)

            def turn(r, i, i_u):
                for k in range(RG):
                    g = r * RG + k
                    dve.wait_ge(gelu_done, g + 1)
                    dve.wait_ge(y_done, g + 1)
                    for j in range(G):
                        ins = dve.tensor_scalar(diag[k][:, j, :], ident[:, :], gel[k][:, j:j + 1],
                                                gate[:, i, bass.ds((r * RG + k) * G + (j - i * SLOTS), 1)], ALU.mult, ALU.mult)
                    ins.then_inc(diag_done, 1)
                    if i_u is not None:
                        for j in range(G):
                            s = u_slot(k, j)
                            ins = dot(s, r * 16 + 16 * (1 + EARLY_SLOT.count(s)), i_u, dots[k][:, j:j + 1])
                        ins.then_inc(dots_done, 1)

            def turns(first, last, i):
                with dve.Fori(first, last) as r:
                    turn(r, i, i)

            def norm_out(i):
                if i == 0:
                    dve.wait_ge(y_done, RG + GROUPS)
                for n in (3, 0, 1, 2):
                    if i and n < 3:
                        dve.wait_ge(bank_done, n + 1)
                    last = dve.bn_stats(stats[:, n, :], ps[4 * i + n][:, :])
                link(last)
                dve.bn_aggr(mv[:, i, :], stats[:, 0:4, :]).then_inc(var2, 1)
                dve.wait_ge(var2, i + 1)
                res = [x1[:, i, n * 512:(n + 1) * 512] for n in range(4)]
                dve.wait_ge(row2_copied, 8)
                for n in range(4):
                    dve.scalar_tensor_tensor(out=res[n], in0=ps[4 * i + n][:, :], scalar=mv[:, i, 0:1],
                                             in1=rows[:, 0, n * 512:(n + 1) * 512], op0=ALU.subtract, op1=ALU.mult)
                dve.wait_ge(sd2, i + 1)
                link(dve.reciprocal(rstd[:, i:i + 1], sd[:, i:i + 1]))
                for n in range(4):
                    dve.scalar_tensor_tensor(out=res[n], in0=res[n], scalar=rstd[:, i:i + 1],
                                             in1=rows[:, 1, n * 512:(n + 1) * 512], op0=ALU.mult, op1=ALU.add).then_inc(res_done, 1)

            per = TURNS // PH
            for h in range(PH - 1):
                turns(h * per, (h + 1) * per, 0)
                if h == 0:
                    gates(0, PH // 2, PH)
                for h1 in (h,) if h < PH - 2 else (h, h + 1):
                    retrieve(1, (h1,), lambda h, c: later[:, (2 * h + c) * PK:(2 * h + c + 1) * PK])
            turns((PH - 1) * per, TURNS - 1, 0)
            turn(TURNS - 1, 0, 1)
            gates(1, 0, PH)
            turns(TURNS, TURNS + 2, 1)
            norm_out(0)
            turns(TURNS + 2, TI * TURNS - 1, 1)
            turn(TI * TURNS - 1, 1, None)
            for k in range(RG):
                last = dve.tensor_tensor(weight[k][:, :], gel[k][:, :], gate[:, 1, SLOTS - (RG - k) * G:][:, 0:G], ALU.mult)
            link(last)
            for s in range(RG * G):
                dve.wait_ge(v_in[s], 16 * TI * TURNS)
                link(dve.scalar_tensor_tensor(out=ps[7][:, :], in0=v_ring[s][:, 1536:2048], scalar=weight[s // G][:, s % G:s % G + 1],
                                              in1=ps[7][:, :], op0=ALU.mult, op1=ALU.add))
            norm_out(1)


def _bucket_onehot():
    half = BUCKETS // 2
    d = np.maximum(S - 1 - np.arange(SKEW), 0)
    large = half + (np.log(np.maximum(d, 1).astype(np.float32) / np.float32(half))
                    / np.float32(np.log(MAX_DIST / half)) * np.float32(BUCKETS - half)).astype(np.int32)
    b = np.where(d < half, d, np.minimum(large, BUCKETS - 1))
    return (np.arange(BUCKETS)[:, None] == b[None, :]).astype(np.float32)


def kernel(x, w_in, w_out, b_out, dw_w, dw_b, conv_ln_g, conv_ln_b, rel_bias,
           ln1_g, ln1_b, peer_wq, peer_sub_keys, peer_u, peer_v, ln2_g, ln2_b):
    import concourse.bacc as _bacc
    from concourse.bass_utils import run_bass_kernel_spmd as _run

    def tiles(w):
        return np.asarray(w).reshape(KC, P, -1, P).transpose(2, 1, 0, 3).reshape(-1, P, UNIT)

    def strips(w):
        return np.asarray(w).reshape(4, 4, P, -1, 512).transpose(3, 0, 2, 1, 4).reshape(-1, P, UNIT)

    def pair(a, b):
        return np.stack([tiles(a), tiles(b)], 1).reshape(-1, P, UNIT)

    def cols(v, n):
        return np.asarray(v).reshape(n, P).T

    w = np.asarray(w_in)[0]
    c_q, c_k, c_v, c_qi, c_ki, c_wi = 2 * DC, 3 * DC, 4 * DC, 5 * DC, 6 * DC, 6 * DC + HD
    stream = np.concatenate([tiles(w[:, c_qi:c_ki]), pair(w[:, 0:DC], w[:, DC:2 * DC]), strips(w[:, c_v:c_qi]),
                             pair(w[:, c_q:c_k], w[:, c_k:c_v]), strips(np.asarray(w_out)[0]), tiles(np.asarray(peer_wq)[0])])
    k_i, w_i = w[:, c_ki:c_wi], w[:, c_wi:]
    kw = np.concatenate([k_i, w_i], 1).reshape(KC, P, KWCOL).transpose(1, 0, 2)
    x2 = np.asarray(x)[0]
    conv = np.concatenate([np.asarray(dw_w)[0], np.asarray(dw_b)], 0)
    ins = {
        "xT": x2.T.reshape(KC, P, S).transpose(1, 0, 2),
        "x_tok": x2,
        "w_stream": stream,
        "w_kw": kw,
        "w_sub": np.asarray(peer_sub_keys)[0].transpose(3, 0, 1, 2).reshape(P, 2 * PH * PK),
        "conv_p": conv.reshape(TAPS + 1, CC, P).transpose(2, 1, 0).reshape(P, -1),
        "cln": np.concatenate([cols(conv_ln_g, CC), cols(conv_ln_b, CC)], 1),
        "bucket1h": _bucket_onehot(),
        "rel_bias": np.asarray(rel_bias),
        "b_out": np.asarray(b_out),
        "ln1_col": np.stack([cols(ln1_g, KC), cols(ln1_b, KC)]),
        "ln_rows": np.concatenate([np.asarray(a) for a in (ln1_g, ln1_b, ln2_g, ln2_b)], 0),
        "u_tab": np.asarray(peer_u)[0],
        "v_tab": np.asarray(peer_v)[0],
    }
    nc = _bacc.Bacc("TRN2", target_bir_lowering=False, num_devices=1)
    arrays, args = {}, {}
    for name, a in ins.items():
        a = np.ascontiguousarray(a)
        arrays[f"in_{name}"] = a
        args[name] = nc.dram_tensor(f"in_{name}", a.shape, mybir.dt.from_np(a.dtype), kind="ExternalInput").ap()
    args["out"] = nc.dram_tensor("out_dram", (S, D), F32, kind="ExternalOutput").ap()
    layer(nc, **args)
    r = _run(nc, [arrays], core_ids=[0])
    return r.results[0]["out_dram"].reshape(1, S, D)
```
